# Optimizing a Trainium2 kernel written in Bass

```python
import functools
import jax, jax.numpy as jnp
from jax import lax
import numpy as np

D_MODEL = 1024
BATCH = 1
SEQ = 1024
DEPTH = 1
DEC_BATCH = 8
DEC_SEQ = 8
PAST_LEN = 2048
PAGE_SIZE = 128

HEAD_DIM = 64
N_HEADS_ATTN = 8
N_KV_HEADS = 2
HEADS_PER_KV = N_HEADS_ATTN // N_KV_HEADS
D_ATTN = N_HEADS_ATTN * HEAD_DIM
D_KV = N_KV_HEADS * HEAD_DIM
N_BRANCH = 3
N_HEADS_RWKV = 8
D_RWKV = N_HEADS_RWKV * HEAD_DIM
D_MIX = D_ATTN + D_RWKV
ROT_DIM = HEAD_DIM // 4
ROPE_THETA = 500000.0
BLOCK_CMP = 32
STRIDE_CMP = 16
BLOCK_SLC = 64
N_SELECT = 16
N_LOCAL = 2
WINDOW = 512
QBLOCK = 128
RANK_W = 32
RANK_A = 32
RANK_G = 64
D_FF = 4 * D_MODEL
SHIFT_COLS = 3 * D_RWKV + RANK_W + RANK_A + RANK_G
IN_COLS = D_ATTN + 6 * D_KV + N_BRANCH * N_HEADS_ATTN + SHIFT_COLS
NORM_EPS = 1e-6
GN_EPS = 64e-5
NEG = -1e30
FORCED_SCORE = 1e9

kernel_name = 'nsa_rwkv7_hybrid_decode_step'

def _split(x, sizes):
    offs = [int(o) for o in np.cumsum(sizes)[:-1]]
    return jnp.split(x, offs, axis=-1)

def rms_norm(x, g):
    xf = x.astype(jnp.float32)
    y = xf * lax.rsqrt(jnp.mean(xf * xf, axis=-1, keepdims=True) + NORM_EPS)
    return (y * g.astype(jnp.float32)).astype(x.dtype)

def rope_tables(pos):
    inv = ROPE_THETA ** (-(jnp.arange(0, ROT_DIM, 2, dtype=jnp.float32) / ROT_DIM))
    ang = pos.astype(jnp.float32)[:, None] * inv[None, :]
    return jnp.cos(ang), jnp.sin(ang)

def apply_partial_rope(x, cos, sin):
    xr = x[..., :ROT_DIM].astype(jnp.float32)
    x1, x2 = xr[..., :ROT_DIM // 2], xr[..., ROT_DIM // 2:]
    c, s = cos[None, :, None, :], sin[None, :, None, :]
    rot = jnp.concatenate([x1 * c - x2 * s, x2 * c + x1 * s], axis=-1).astype(x.dtype)
    return jnp.concatenate([rot, x[..., ROT_DIM:]], axis=-1)

def masked_softmax(s, mask):
    p = jax.nn.softmax(jnp.where(mask, s, NEG), axis=-1)
    return jnp.where(mask, p, 0.0)

def gather_pages(pool, page_table):
    g = pool[page_table]
    return g.reshape(page_table.shape[0], -1, 2, N_KV_HEADS, HEAD_DIM)

def gather_blocks(blocks, idx):
    return jax.vmap(jax.vmap(lambda b, i: b[i]))(blocks, idx)

def nsa_heads(z_attn, pos, q_norm_g, k_norm_g):
    B, T = z_attn.shape[:2]
    parts = _split(z_attn, [D_ATTN] + [D_KV] * 6)
    cos, sin = rope_tables(pos)
    q = apply_partial_rope(rms_norm(parts[0].reshape(B, T, N_HEADS_ATTN, HEAD_DIM), q_norm_g), cos, sin)
    kvs = []
    for br in range(N_BRANCH):
        k = parts[1 + 2 * br].reshape(B, T, N_KV_HEADS, HEAD_DIM)
        v = parts[2 + 2 * br].reshape(B, T, N_KV_HEADS, HEAD_DIM)
        k = apply_partial_rope(rms_norm(k, k_norm_g[br]), cos, sin)
        kvs.append(jnp.stack([k, v], axis=2))
    return q, kvs

def compress_blocks(kv, cmp_pe, cmp_w):
    B, L = kv.shape[:2]
    n_cmp = (L - BLOCK_CMP) // STRIDE_CMP + 1
    r = BLOCK_CMP // STRIDE_CMP
    n_chunks = n_cmp + r - 1
    chunks = kv[:, :n_chunks * STRIDE_CMP].reshape(B, n_chunks, STRIDE_CMP, 2, N_KV_HEADS, HEAD_DIM)
    pe = cmp_pe.reshape(2, r, STRIDE_CMP, HEAD_DIM)
    w = cmp_w.reshape(2, r, STRIDE_CMP, HEAD_DIM, HEAD_DIM)
    comp = 0.0
    for i in range(r):
        part = chunks[:, i:i + n_cmp] + jnp.moveaxis(pe[:, i], 0, 1)[None, None, :, :, None, :]
        comp = comp + jnp.einsum('bnscgd,csde->bncge', part, w[:, i])
    c_end = jnp.arange(n_cmp, dtype=jnp.int32) * STRIDE_CMP + BLOCK_CMP - 1
    return comp[:, :, 0], comp[:, :, 1], c_end

def cmp_to_slc_map(n_cmp, n_slc):
    start = np.arange(n_cmp) * STRIDE_CMP
    first, last = start // BLOCK_SLC, (start + BLOCK_CMP - 1) // BLOCK_SLC
    j = np.arange(n_slc)
    return jnp.asarray(((first[:, None] <= j[None, :]) & (last[:, None] >= j[None, :])).astype(np.float32))

def to_slc_blocks(kv):
    B, L = kv.shape[:2]
    n_slc = -(-L // BLOCK_SLC)
    kv = jnp.pad(kv, ((0, 0), (0, n_slc * BLOCK_SLC - L), (0, 0), (0, 0), (0, 0)))
    return kv.reshape(B, n_slc, BLOCK_SLC, 2, N_KV_HEADS, HEAD_DIM).transpose(0, 4, 1, 2, 3, 5)

def nsa_query_block(q, q_pos, kc, vc, c_end, sel_map, slc_blocks, win_kv, w_pos, gates):
    B, Tq = q.shape[:2]
    f32 = jnp.float32
    qg = q.astype(f32).reshape(B, Tq, N_KV_HEADS, HEADS_PER_KV, HEAD_DIM) * (HEAD_DIM ** -0.5)
    s_c = jnp.einsum('bqghd,bngd->bghqn', qg, kc.astype(f32))
    p_c = masked_softmax(s_c, c_end[None, :] <= q_pos[:, None])
    o_c = jnp.einsum('bghqn,bngd->bqghd', p_c, vc.astype(f32))
    n_slc = slc_blocks.shape[2]
    imp = jnp.einsum('bghqn,ns->bgqs', p_c, sel_map)
    j = jnp.arange(n_slc, dtype=jnp.int32)[None, :]
    cur = (q_pos // BLOCK_SLC)[:, None]
    forced = (j == 0) | ((j <= cur) & (j > cur - N_LOCAL))
    causal = j * BLOCK_SLC <= q_pos[:, None]
    imp = jnp.where(causal, jnp.where(forced, FORCED_SCORE, imp), NEG)
    n_sel = min(N_SELECT, n_slc)
    _, idx = lax.top_k(imp, n_sel)
    g_kv = gather_blocks(slc_blocks, idx.reshape(B, N_KV_HEADS, Tq * n_sel))
    g_kv = g_kv.reshape(B, N_KV_HEADS, Tq, n_sel * BLOCK_SLC, 2, HEAD_DIM).astype(f32)
    k_pos = (idx[..., None] * BLOCK_SLC + jnp.arange(BLOCK_SLC, dtype=jnp.int32)).reshape(B, N_KV_HEADS, Tq, n_sel * BLOCK_SLC)
    s_s = jnp.einsum('bqghd,bgqkd->bghqk', qg, g_kv[..., 0, :])
    p_s = masked_softmax(s_s, (k_pos <= q_pos[:, None])[:, :, None])
    o_s = jnp.einsum('bghqk,bgqkd->bqghd', p_s, g_kv[..., 1, :])
    s_w = jnp.einsum('bqghd,bkgd->bghqk', qg, win_kv[:, :, 0].astype(f32))
    dist = q_pos[:, None] - w_pos[None, :]
    p_w = masked_softmax(s_w, (dist >= 0) & (dist < WINDOW) & (w_pos[None, :] >= 0))
    o_w = jnp.einsum('bghqk,bkgd->bqghd', p_w, win_kv[:, :, 1].astype(f32))
    g = gates.astype(f32).reshape(B, Tq, N_KV_HEADS, HEADS_PER_KV, N_BRANCH)
    o = g[..., 0:1] * o_c + g[..., 1:2] * o_s + g[..., 2:3] * o_w
    return o.reshape(B, Tq, D_ATTN).astype(q.dtype)

def prompt_attention(q, kvs, gates, lp):
    B, T = q.shape[:2]
    kc, vc, c_end = compress_blocks(kvs[0], lp['cmp_pe'], lp['cmp_w'])
    slc_blocks = to_slc_blocks(kvs[1])
    sel_map = cmp_to_slc_map(kc.shape[1], slc_blocks.shape[2])
    win_pad = jnp.pad(kvs[2], ((0, 0), (WINDOW, 0), (0, 0), (0, 0), (0, 0)))

    def one_query_block(q0):
        q_pos = q0 + jnp.arange(QBLOCK, dtype=jnp.int32)
        w_pos = q0 - WINDOW + jnp.arange(WINDOW + QBLOCK, dtype=jnp.int32)
        return nsa_query_block(
            lax.dynamic_slice_in_dim(q, q0, QBLOCK, axis=1), q_pos, kc, vc, c_end, sel_map, slc_blocks,
            lax.dynamic_slice_in_dim(win_pad, q0, WINDOW + QBLOCK, axis=1), w_pos,
            lax.dynamic_slice_in_dim(gates, q0, QBLOCK, axis=1))

    out = lax.map(one_query_block, jnp.arange(0, T, QBLOCK, dtype=jnp.int32))
    out = jnp.moveaxis(out, 0, 1).reshape(B, T, D_ATTN)
    cmp_pages = kvs[0].reshape(B, T // PAGE_SIZE, PAGE_SIZE, 2, N_KV_HEADS, HEAD_DIM)
    slc_pages = kvs[1].reshape(B, T // PAGE_SIZE, PAGE_SIZE, 2, N_KV_HEADS, HEAD_DIM)
    return out, (cmp_pages, slc_pages, kvs[2][:, -min(WINDOW, T):])

def sample_attention(q, kvs, gates, lp, cache_cmp, cache_slc, cache_win, page_table):
    Tn = q.shape[1]
    past = page_table.shape[1] * PAGE_SIZE
    w_buf = cache_win.shape[1]
    full_cmp = jnp.concatenate([gather_pages(cache_cmp, page_table), kvs[0]], axis=1)
    full_slc = jnp.concatenate([gather_pages(cache_slc, page_table), kvs[1]], axis=1)
    win = jnp.concatenate([cache_win, kvs[2]], axis=1)
    kc, vc, c_end = compress_blocks(full_cmp, lp['cmp_pe'], lp['cmp_w'])
    slc_blocks = to_slc_blocks(full_slc)
    sel_map = cmp_to_slc_map(kc.shape[1], slc_blocks.shape[2])
    q_pos = past + jnp.arange(Tn, dtype=jnp.int32)
    w_pos = past - w_buf + jnp.arange(w_buf + Tn, dtype=jnp.int32)
    out = nsa_query_block(q, q_pos, kc, vc, c_end, sel_map, slc_blocks, win, w_pos, gates)
    return out, (kvs[0], kvs[1], win[:, -w_buf:])

def rwkv7_time_mix(zs, shift_prev, wkv0, v_first, lp):
    f32 = jnp.float32
    B, T = zs.shape[:2]
    zf = zs.astype(f32)
    prev = jnp.concatenate([shift_prev.astype(f32)[:, None], zf[:, :-1]], axis=1)
    xs = zf + (prev - zf) * lp['mu']
    r, k, v, xw, xa, xg = _split(xs, [D_RWKV] * 3 + [RANK_W, RANK_A, RANK_G])
    w_raw = -jax.nn.softplus(-(lp['w0'] + jnp.tanh(xw) @ lp['w2'])) - 0.5
    decay = jnp.exp(-jnp.exp(w_raw))
    a = jax.nn.sigmoid(lp['a0'] + xa @ lp['a2'])
    if lp['vres'] is None:
        v_first = v
    else:
        vres0, vres2 = lp['vres']
        v = v + (v_first - v) * jax.nn.sigmoid(vres0 + xa @ vres2)
    g = jax.nn.sigmoid(xg) @ lp['g2']
    heads = lambda t: t.reshape(B, T, N_HEADS_RWKV, HEAD_DIM)
    kk = heads(k * lp['k_k'])
    kk = kk * lax.rsqrt(jnp.maximum(jnp.sum(kk * kk, axis=-1, keepdims=True), 1e-24))
    k = k * (1.0 + (a - 1.0) * lp['k_a'])
    r_h, k_h, v_h, a_h, d_h = heads(r), heads(k), heads(v), heads(a), heads(decay)

    def step(S, inp):
        r_t, d_t, kk_t, a_t, k_t, v_t = inp
        sa = jnp.einsum('bhvk,bhk->bhv', S, -kk_t)
        S = S * d_t[:, :, None, :] + sa[..., None] * (kk_t * a_t)[:, :, None, :] + v_t[..., None] * k_t[:, :, None, :]
        return S, jnp.einsum('bhvk,bhk->bhv', S, r_t)

    tm = lambda t: jnp.moveaxis(t, 1, 0)
    S_T, ys = lax.scan(step, wkv0.astype(f32), (tm(r_h), tm(d_h), tm(kk), tm(a_h), tm(k_h), tm(v_h)))
    y = jnp.moveaxis(ys, 0, 1)
    mean = jnp.mean(y, axis=-1, keepdims=True)
    var = jnp.mean(jnp.square(y - mean), axis=-1, keepdims=True)
    y = (y - mean) * lax.rsqrt(var + GN_EPS) * lp['lnx_w'].reshape(N_HEADS_RWKV, HEAD_DIM) + lp['lnx_b'].reshape(N_HEADS_RWKV, HEAD_DIM)
    y = y + jnp.sum(r_h * k_h * lp['r_k'], axis=-1, keepdims=True) * v_h
    y = y.reshape(B, T, D_RWKV) * g
    return y, S_T, zs[:, -1], v_first

def trunk_layer(x, pos, attn_fn, shift_prev, wkv0, v_first, lp):
    n = rms_norm(x, lp['norm1_g'])
    z = n @ lp['w_in']
    z_attn, z_gate, z_rwkv = _split(z, [D_ATTN + 6 * D_KV, N_BRANCH * N_HEADS_ATTN, SHIFT_COLS])
    q, kvs = nsa_heads(z_attn, pos, lp['q_norm_g'], lp['k_norm_g'])
    gates = jax.nn.sigmoid((z_gate + lp['gate_b']).astype(jnp.float32))
    o_attn, attn_state = attn_fn(q, kvs, gates, lp)
    o_rwkv, wkv_t, shift_t, v_first = rwkv7_time_mix(z_rwkv, shift_prev, wkv0, v_first, lp)
    mixed = jnp.concatenate([o_attn, o_rwkv.astype(o_attn.dtype)], axis=-1)
    h = x + (mixed @ lp['w_out']).astype(x.dtype)
    n2 = rms_norm(h, lp['norm2_g'])
    y = h + (jnp.square(jax.nn.relu(n2 @ lp['w_up'])) @ lp['w_down']).astype(x.dtype)
    return y, attn_state, wkv_t, shift_t, v_first

def setup_inputs(seed: int = 0) -> dict:
    key = jax.random.key(seed)
    ks = iter(jax.random.split(key, 40))
    f32 = jnp.float32
    nrm = lambda shape, s: jax.random.normal(next(ks), shape, f32) * s
    uni = lambda shape, lo, hi: jax.random.uniform(next(ks), shape, f32, lo, hi)
    n_pages = PAST_LEN // PAGE_SIZE
    used = DEC_BATCH * n_pages
    n_pool = used + max(1, used // 4)
    w_buf = min(WINDOW, PAST_LEN)
    pool_shape = (DEPTH, n_pool, PAGE_SIZE, 2, N_KV_HEADS, HEAD_DIM)
    return {
        'x_prompt': nrm((BATCH, SEQ, D_MODEL), 1.0),
        'x_sample': nrm((DEC_BATCH, DEC_SEQ, D_MODEL), 1.0),
        'cache_cmp_kv': nrm(pool_shape, 1.0),
        'cache_slc_kv': nrm(pool_shape, 1.0),
        'cache_win_kv': nrm((DEPTH, DEC_BATCH, w_buf, 2, N_KV_HEADS, HEAD_DIM), 1.0),
        'state_wkv': nrm((DEPTH, DEC_BATCH, N_HEADS_RWKV, HEAD_DIM, HEAD_DIM), 1.0),
        'state_shift': nrm((DEPTH, DEC_BATCH, SHIFT_COLS), 1.0),
        'page_table': jax.random.permutation(next(ks), n_pool)[:used].reshape(DEC_BATCH, n_pages).astype(jnp.int32),
        'norm1_g': 1.0 + nrm((DEPTH, D_MODEL), 0.02),
        'w_in': nrm((DEPTH, D_MODEL, IN_COLS), D_MODEL ** -0.5),
        'q_norm_g': 1.0 + nrm((DEPTH, HEAD_DIM), 0.02),
        'k_norm_g': 1.0 + nrm((DEPTH, N_BRANCH, HEAD_DIM), 0.02),
        'gate_b': nrm((DEPTH, N_BRANCH * N_HEADS_ATTN), 0.1),
        'cmp_pe': nrm((DEPTH, 2, BLOCK_CMP, HEAD_DIM), 0.1),
        'cmp_w': nrm((DEPTH, 2, BLOCK_CMP, HEAD_DIM, HEAD_DIM), (BLOCK_CMP * HEAD_DIM) ** -0.5),
        'shift_mu': uni((DEPTH, SHIFT_COLS), 0.0, 1.0),
        'w0': uni((DEPTH, D_RWKV), -5.0, 0.0),
        'w2': nrm((DEPTH, RANK_W, D_RWKV), 0.1 * RANK_W ** -0.5),
        'a0': nrm((DEPTH, D_RWKV), 0.1),
        'a2': nrm((DEPTH, RANK_A, D_RWKV), 0.5 * RANK_A ** -0.5),
        'vres0': nrm((DEPTH - 1, D_RWKV), 0.1),
        'vres2': nrm((DEPTH - 1, RANK_A, D_RWKV), 0.5 * RANK_A ** -0.5),
        'g2': nrm((DEPTH, RANK_G, D_RWKV), RANK_G ** -0.5),
        'k_k': 0.85 + nrm((DEPTH, D_RWKV), 0.05),
        'k_a': 1.0 + nrm((DEPTH, D_RWKV), 0.05),
        'r_k': nrm((DEPTH, N_HEADS_RWKV, HEAD_DIM), 0.1),
        'lnx_w': 1.0 + nrm((DEPTH, D_RWKV), 0.02),
        'lnx_b': nrm((DEPTH, D_RWKV), 0.02),
        'w_out': nrm((DEPTH, D_MIX, D_MODEL), D_MIX ** -0.5),
        'norm2_g': 1.0 + nrm((DEPTH, D_MODEL), 0.02),
        'w_up': nrm((DEPTH, D_MODEL, D_FF), D_MODEL ** -0.5),
        'w_down': nrm((DEPTH, D_FF, D_MODEL), D_FF ** -0.5),
    }

def reference(x_prompt, x_sample, cache_cmp_kv, cache_slc_kv, cache_win_kv, state_wkv, state_shift, page_table,
              norm1_g, w_in, q_norm_g, k_norm_g, gate_b, cmp_pe, cmp_w, shift_mu, w0, w2, a0, a2, vres0, vres2,
              g2, k_k, k_a, r_k, lnx_w, lnx_b, w_out, norm2_g, w_up, w_down):
    B, T = x_prompt.shape[:2]
    Tn = x_sample.shape[1]
    past = page_table.shape[1] * PAGE_SIZE
    pos_p = jnp.arange(T, dtype=jnp.int32)
    pos_s = past + jnp.arange(Tn, dtype=jnp.int32)
    shift_zero = jnp.zeros((B, SHIFT_COLS), x_prompt.dtype)
    wkv_zero = jnp.zeros((B, N_HEADS_RWKV, HEAD_DIM, HEAD_DIM), jnp.float32)
    xp, xs = x_prompt, x_sample
    vf_p, vf_s = None, None
    p_cmp, p_slc, p_win, p_wkv, p_shift = [], [], [], [], []
    s_cmp, s_slc, s_win, s_wkv, s_shift = [], [], [], [], []
    for l in range(DEPTH):
        lp = {'norm1_g': norm1_g[l], 'w_in': w_in[l], 'q_norm_g': q_norm_g[l], 'k_norm_g': k_norm_g[l],
              'gate_b': gate_b[l], 'cmp_pe': cmp_pe[l], 'cmp_w': cmp_w[l], 'mu': shift_mu[l], 'w0': w0[l],
              'w2': w2[l], 'a0': a0[l], 'a2': a2[l],
              'vres': None if l == 0 else (vres0[l - 1], vres2[l - 1]),
              'g2': g2[l], 'k_k': k_k[l], 'k_a': k_a[l], 'r_k': r_k[l], 'lnx_w': lnx_w[l], 'lnx_b': lnx_b[l],
              'w_out': w_out[l], 'norm2_g': norm2_g[l], 'w_up': w_up[l], 'w_down': w_down[l]}
        xp, (c_kv, sl_kv, w_kv), wkv_t, sh_t, vf_p = trunk_layer(
            xp, pos_p, prompt_attention, shift_zero, wkv_zero, vf_p, lp)
        p_cmp.append(c_kv); p_slc.append(sl_kv); p_win.append(w_kv); p_wkv.append(wkv_t); p_shift.append(sh_t)
        sample_fn = functools.partial(sample_attention, cache_cmp=cache_cmp_kv[l], cache_slc=cache_slc_kv[l],
                                      cache_win=cache_win_kv[l], page_table=page_table)
        xs, (c_kv, sl_kv, w_kv), wkv_t, sh_t, vf_s = trunk_layer(
            xs, pos_s, sample_fn, state_shift[l], state_wkv[l], vf_s, lp)
        s_cmp.append(c_kv); s_slc.append(sl_kv); s_win.append(w_kv); s_wkv.append(wkv_t); s_shift.append(sh_t)
    return (xp, xs, jnp.stack(p_cmp), jnp.stack(p_slc), jnp.stack(p_win), jnp.stack(p_wkv), jnp.stack(p_shift),
            jnp.stack(s_cmp), jnp.stack(s_slc), jnp.stack(s_win), jnp.stack(s_wkv), jnp.stack(s_shift))


_drawn_inputs = setup_inputs


def setup_inputs(seed=0):
    import zlib

    import numpy as np

    out = dict(_drawn_inputs(seed))
    spreads = {}
    factors = {'cache_slc_kv': 2.746,
     'q_norm_g': 8.0,
     'k_norm_g': 3.563,
     'gate_b': 8.0,
     'w2': 8.0,
     'lnx_w': 21.385,
     'lnx_b': 57.391,
     'norm2_g': 9.966,
     'cmp_pe': 4.181,
     'r_k': 4.631}
    for name, (base, spread) in spreads.items():
        noise = np.random.default_rng([zlib.crc32(name.encode()), seed]).standard_normal(out[name].shape)
        drawn = base * np.exp(spread * noise) if base else spread * noise
        out[name] = __import__('jax').numpy.asarray(drawn.astype(out[name].dtype))
    for name, factor in factors.items():
        out[name] = (out[name] * factor).astype(out[name].dtype)
    return out
```

```python
from contextlib import ExitStack
import math

import concourse.bass as bass
from concourse import mybir

F32 = mybir.dt.float32
I32 = mybir.dt.int32
ALU = mybir.AluOpType
ACT = mybir.ActivationFunctionType
AX = mybir.AxisListType

P = 128
D_MODEL, SEQ, DEC_B, DEC_T = 1024, 1024, 8, 8
PAST, PAGE, HD, HEADS, KVH = 2048, 128, 64, 8, 2
HG = HEADS // KVH
D_ATTN, D_KV = HEADS * HD, KVH * HD
ROT = HD // 4
WINDOW, BLOCK, STRIDE, SLC, NSEL = 512, 32, 16, 64, 16
RW = 512
ZA = D_ATTN + 6 * D_KV + 3 * HEADS
ZR = 3 * RW + 128
D_FF = 4 * D_MODEL
KT = D_MODEL // P
PT = SEQ // P
TILES = PT + 1
NS = DEC_B * DEC_T
TOK = SEQ + NS
RC = ZR // P
HP = 4
CH = 64
NCH = SEQ // CH
GATE0 = D_ATTN + 6 * D_KV
NPG = PAST // PAGE
NEG = -1e30
KAPPA = math.exp(-0.5)
NCMP = (PAST - BLOCK) // STRIDE + 1
NCMP_P = (SEQ - BLOCK) // STRIDE + 1
NBLK = -(-(PAST + DEC_T) // SLC)
LEVELS = (2, 4, 8, 16, 32)


def rows(t):
    return P if t < PT else NS


def decode_trunk(nc, x_prompt, x_sample, cache_cmp_kv, cache_slc_kv, cache_win_kv, state_wkv, state_shift,
                 page_table, norm1_g, w_in, q_norm_g, k_norm_g, gate_b, cmp_pe, cmp_w, shift_mu, w0, w2, a0, a2,
                 g2, k_k, k_a, r_k, lnx_w, lnx_b, w_out, norm2_g, w_up, w_down, rope,
                 y_prompt, y_sample, prompt_cmp, prompt_slc, prompt_win, prompt_wkv, prompt_shift,
                 sample_cmp, sample_slc, sample_win, sample_wkv, sample_shift):
    ctx = ExitStack()
    with ctx:
        sems = {}

        def sem(name):
            if name not in sems:
                sems[name] = ctx.enter_context(nc.semaphore(name))
            return sems[name]

        ONCE = {"pool_once": ["iotas", "ident_ready", "masks_ready", "spread_ready"],
                "pe_once": ["shift_turned", "last_turned", "rw_pstate", "pe_sum", "sq_turned", "gs_spread", "so_turned"],
                "dve_once": ["last_cols", "shift_out", "rw_st0", "rw_prompt_done", "rw_all_done", "pe_bias", "q_zero", "pa_done"],
                "act_once": ["rw_pstate_rows", "egates", "sq_ready", "att_all_done"]}

        def once(name):
            for engine, names in ONCE.items():
                if name in names:
                    return sem(engine), names.index(name) + 1

        def sb(name, *dims, dt=F32):
            t = ctx.enter_context(nc.sbuf_tensor(name, [P, math.prod(dims)], dt))
            return shaped(t[:, :], *dims)

        def shaped(flat, *dims):
            names = "abcd"[:len(dims)]
            if len(dims) == 1:
                return flat
            return flat.rearrange(f"p ({' '.join(names)}) -> p {' '.join(names)}",
                                  **{n: d for n, d in zip(names, dims)})

        def spread(ap, axis, n):
            v = ap.unsqueeze(axis)
            shape = list(v.shape)
            shape[axis] = n
            return v.broadcast_to(shape)

        ident = sb("ident", P)
        block_ones = sb("block_ones", P)
        causal_add = sb("causal_add", P)
        edge_add = sb("edge_add", P)
        cmp_keep = sb("cmp_keep", PT, NCMP_P)
        cmp_add = sb("cmp_add", PT, NCMP_P)
        scan_keep = sb("scan_keep", 2, HP * CH)
        m_a = sb("m_a", 2, CH)
        m_t = sb("m_t", 2, 2, CH)
        m_one = sb("m_one", CH)
        m_onet = sb("m_onet", CH)
        m_lev = sb("m_lev", len(LEVELS), CH)
        row_of = sb("row_of", DEC_B)
        head_sum = sb("head_sum", P)
        before = sb("before", NBLK, NBLK)
        tail_add = sb("tail_add", DEC_T)
        first_add = sb("first_add", DEC_T)
        num = sb("num", 8)
        e_scale = sb("e_scale", 3)
        gq = sb("gq", HD)
        gk = sb("gk", 3, HD)
        gb = sb("gb", 3 * HEADS)
        lnw = sb("lnw", HP, HD)
        lnb = sb("lnb", HP, HD)
        g1 = sb("g1", KT)
        g2n = sb("g2n", KT)
        mu = sb("mu", RC)
        w0a0 = sb("w0a0", 2 * HP)
        kkv = sb("kkv", HP)
        kav = sb("kav", 2, HP)
        rkv = sb("rkv", HP)
        lora = sb("lora", RW)
        rope_t = sb("rope_t", TILES, 2, ROT)
        pages = ctx.enter_context(nc.sbuf_tensor("pages", [1, DEC_B * NPG], I32))
        eps_c, gneps_c = num[:, 0:1], num[:, 1:2]

        ARENA = 46990
        arena = ctx.enter_context(nc.sbuf_tensor("arena", [P, ARENA], F32))

        def region(at, *dims):
            n = math.prod(dims)
            assert at + n <= ARENA, (at, dims)
            return shaped(arena[:, at:at + n], *dims)

        Z0 = 0
        R0 = Z0 + TILES * ZA
        S0 = R0 + RC * (SEQ + 1)
        N0 = S0 + RC * DEC_B * (DEC_T + 1)
        W0 = N0 + KT * TOK
        za = region(Z0, TILES, ZA)
        rt = region(R0, RC, SEQ + 1)
        zs = region(S0, RC, DEC_B, DEC_T + 1)
        nt = region(N0, KT, TOK)
        mixed = nt
        wb = [region(W0 + i * KT * 512, KT, 512) for i in range(2)]
        xb = [region(W0 + 2 * KT * 512 + i * D_MODEL, D_MODEL) for i in range(2)]
        xn = [region(W0 + 2 * KT * 512 + (2 + i) * D_MODEL, D_MODEL) for i in range(2)]
        stat = sb("stat", 4 * TILES)

        psum = ctx.enter_context(nc.psum_tensor("psum", [P, 4096], F32))[:, :]
        banks = [psum[:, 512 * i:512 * i + 512] for i in range(8)]

        X0 = W0 + 2 * KT * 512
        sq_a, sq_b = region(X0, HEADS, HD), region(X0 + 512, 3, KVH, HD)
        ra, rb = region(X0 + 896, HEADS, ROT), region(X0 + 1024, HEADS, ROT)
        head_rs = region(X0 + 1152, 2, HEADS + 3 * KVH)
        last_cols = region(X0 + 1200, RC, DEC_B + 1)
        shift_raw = region(X0 + 1320, ZR)
        shift_rows = shift_raw
        I0 = Z0 + PT * ZA
        it_col, it_col8, it_col5 = (region(I0 + i * P, P).bitcast(I32) for i in range(3))
        col8, row85 = region(I0 + 3 * P, P), region(I0 + 4 * P, 2)
        it_row, it_row2 = region(I0 + 4 * P + 2, 1).bitcast(I32), region(I0 + 4 * P + 3, 2).bitcast(I32)
        stores = [0]
        CONSTS = 20

        at = [W0, N0]

        def work(*dims, pool=0):
            v = region(at[pool], *dims)
            at[pool] += math.prod(dims)
            return v

        def ring(*dims, pool=0):
            return [work(*dims, pool=pool) for _ in range(3)]
        xs = work(RC, CH)
        ebuf, lbuf = work(CH), work(CH)
        kkraw, sqk = work(HP, CH), work(HP, CH)
        kkn, ssm = kkraw, sqk
        sig = work(2, HP, CH)
        cs, cx = work(HP, CH), work(HP, CH)
        dprev, dinv = cx, work(HP, CH)
        kka, kmod, tmp = (work(HP, CH) for _ in range(3))
        rkk = tmp
        bk = work(HP, 2, CH)
        amat = work(HP, CH)
        xsb = work(HP, CH)
        amt = work(2, HP, CH)
        wsb, nu, yc, bv = (work(HP, CH) for _ in range(4))
        sqy = wsb
        ystat = work(2, HP)
        st = work(HP, HD)
        dec_r = ring(HP, CH)
        pr_r = ring(HP, 2, CH)
        atrb_r = ring(HP, 2, CH)
        gtrk_r = ring(HP, 2, CH)
        bonus_r = ring(HP)
        vtok_r = ring(HP, CH, pool=1)
        gtok_r = ring(HP, CH, pool=1)
        tokbk_r = ring(2, HP, CH, pool=1)
        tu_r = [work(HP, 2, CH, pool=1) for _ in range(2)] + [work(HP, 2, CH)]
        assert at[0] <= ARENA and at[1] <= N0 + HP * TOK, (at, ARENA, N0 + HP * TOK)
        st_rows = region(W0, HP, P)
        sst = region(R0, HP, DEC_B, HD)
        nub = region(R0 + 2048, HP, DEC_B, HD)
        vb = region(R0 + 4096, HP, DEC_B, HD)
        s0raw = region(R0 + 6144, DEC_B, HEADS * HD)
        sst_rows = s0raw
        pst = region(R0 + 10240, HP, 2, CH)
        st_rows = region(R0 + 10752, HP, P)
        SBANK = (0, 1, 2, 4)

        def nlev(c):
            return len(LEVELS) if c < NCH else 2

        def lev0(c):
            return len(LEVELS) * c
        HALVES = (slice(0, 64), slice(64, 128))
        TICKS = (16, 10, 6)

        def staged(f, l, y):
            for n in range(NCH + 3):
                now = [(g(n - d), k) for d, (g, k) in enumerate(zip((f, l, y), TICKS)) if 0 <= n - d <= NCH]
                for tick in range(TICKS[0]):
                    for g, k in reversed(now):
                        if (tick + 1) * k // TICKS[0] > tick * k // TICKS[0]:
                            next(g)
        at[0] = W0
        kc_all = work(1 + DEC_B, P)
        vc_all = work(1 + DEC_B, KVH, HD)
        ktp = work(2, TOK)
        qs = work(DEC_B, HG, DEC_T)
        vnew = work(DEC_B, 2, D_KV)
        gates = work(TILES, 3 * HEADS)
        gs = work(DEC_B // 2, 3)
        spread_rows = work(DEC_B // 2, P)
        gtmp = work(3, HEADS)
        osum = work(DEC_B // 2, HD)
        W1 = at[0]
        pmax, psum_ = work(4), work(4)
        c8 = work(3, HEADS)
        oacc = [work(HEADS, HD) for _ in range(2)]
        assert at[0] <= ARENA
        at[0] = R0
        chunk_flat = [work(STRIDE * 2 * D_KV) for _ in range(2)]
        by_head = work(2 * KVH, STRIDE, HD)
        xt = [work(2, KVH, P) for _ in range(2)]
        assert at[0] <= N0
        at[0] = W1
        xt += [work(2, KVH, P) for _ in range(2)]
        ycmp = work(2, KVH, P)
        wcmp = work(2, STRIDE // 2, 2, HD)
        pecol = work(2, 2, STRIDE // 2)
        pebias = work(2)
        assert at[0] <= ARENA
        at[0] = R0
        pbuf = [work(1024) for _ in range(2)]
        ptb = [work(512) for _ in range(4)]
        qt = [work(KVH, HG, P) for _ in range(2)]
        assert at[0] <= N0
        at[0] = R0
        ctok = work(NPG, 2 * D_KV)
        ktb = work(PAST)
        vtok2 = work(2, NPG, D_KV)
        ssel = work(PAST + DEC_T)
        swin = work(WINDOW + DEC_T)
        swk = [work(WINDOW) for _ in range(2)]
        assert at[0] <= N0
        at[0] = W1
        wtok = work(2, 4, 2 * D_KV)
        pcs = work(P + 1)
        imp = work(NBLK)
        rank_eq = work(NBLK, NBLK)
        rank_gt = shaped(ssel[:, 0:NBLK * NBLK], NBLK, NBLK)
        sst4 = work(4)
        ptn = work(2, P)
        ptn_c = work(P)
        assert at[0] <= ARENA, at[0]

        NG, GF = 4, KT
        y = region(0, TILES, D_MODEL)
        wo = wup = region(TILES * D_MODEL, KT, D_MODEL)
        act_p = region(TILES * D_MODEL + KT * D_MODEL, GF, SEQ)
        assert TILES * D_MODEL + KT * D_MODEL + GF * SEQ <= N0
        at[0] = W0
        wdn = work(GF, D_MODEL)
        x2 = [work(D_MODEL) for _ in range(2)]
        hn = work(D_MODEL)
        act_s = work(GF, NS)

        def act_of(f, s):
            a, w = SPANS[s]
            return act_p[:, f, a:a + w] if s < 2 else act_s[:, f, :]

        NSEQ = 1 + DEC_B

        def head_rows(u, c):
            n = SEQ // STRIDE if u == 0 else P
            part = slice(KVH * c, KVH * (c + 1))
            return (by_head[0:n, part].rearrange("p c s d -> p s c d"),
                    shaped(chunk_flat[u % 2][0:n], STRIDE, 2 * KVH, HD)[:, :, part, :])

        def chunk_loads(u):
            return 16 * (1 + NPG * (u // 2)) if u % 2 == 0 else 16 * NPG * (u // 2 + 1)
        units = []
        for i in range(PT):
            units.append((i, "c", None))
            for h in range(HEADS):
                units += [(i, "s", h), (i, "w", h)]
        UPT = 1 + 2 * HEADS

        def key_tiles(u):
            i, kind, _ = units[u]
            return list(range(max(0, i - WINDOW // P) if kind == "w" else 0, i + 1))

        def parts_of(u):
            ks = list(range(HEADS)) if units[u][1] == "c" else key_tiles(u)
            return [ks[j:j + 4] for j in range(0, len(ks), 4)]

        events = []
        for n in range(len(units) + 6):
            i, r = divmod(n + 2, UPT)
            if n == 0:
                events.append(("q", 0))
            elif r == 0 and i < PT:
                events.append(("q", i))
            if n < len(units):
                events.append(("S", n))
            if 1 <= n <= len(units):
                events += [("T", n - 1, j) for j in range(len(parts_of(n - 1)))]
            if 2 <= n < len(units) + 2:
                events.append(("O", n - 2))
            i, r = divmod(n - 4, UPT)
            if n >= 5 and r == UPT - 1 and i < PT:
                events.append(("m", i))
        turns = [e for e in events if e[0] in "qTm"]
        turn_no = {e: f for f, e in enumerate(turns)}
        tparts = [e for e in turns if e[0] == "T"]
        slot_no = {e: f for f, e in enumerate(tparts)}
        slot_owner = [e[1] for e in tparts]

        def turn_copy(e, eng, copy):
            b = banks[4 + turn_no[e] % 2]
            if e[0] == "q":
                if e[1] >= 2:
                    eng.wait_ge(sem("pa_s"), UPT * (e[1] - 1))
                for g in range(KVH):
                    ins = copy(qt[e[1] % 2][HALVES[g], g], shaped(b, HG, P)[HALVES[g]], HD ** -0.5)
                return ins
            if e[0] == "m":
                return copy(mixed[:, 0:HP, e[1] * P:(e[1] + 1) * P], shaped(b, HP, P), 1.0)
            _, u, j = e
            s = slot_no[e]
            if s >= 4:
                eng.wait_ge(sem("pa_o"), slot_owner[s - 4] + 1)
            n = P * len(parts_of(u)[j])
            p0 = NCMP_P if units[u][1] == "c" else P
            return copy(ptb[s % 4][0:p0, 0:n], b[0:p0, 0:n], 1.0)

        def vcols(br, g):
            c0 = D_ATTN + 2 * D_KV * br + D_KV + HD * g
            return slice(c0, c0 + HD)
        block = ctx.enter_context(nc.Block())

        BLOCKS = [(0, 512), (512, 512), (1024, ZA - 1024)] + [(ZA + 512 * i, min(512, ZR - 512 * i)) for i in range(4)]
        ATT_BLOCKS = 3
        SPANS = [(0, 512), (512, 512), (1024, NS)]
        PROJ = [(b, t, None) for b in range(ATT_BLOCKS) for t in range(TILES)]
        PROJ += [(b, c, s) for b in range(ATT_BLOCKS, len(BLOCKS)) for c in range(BLOCKS[b][1] // P) for s in range(3)]
        last_of_block = [max(i for i, p in enumerate(PROJ) if p[0] == b) for b in range(len(BLOCKS))]
        att_done = ATT_BLOCKS * TILES

        def linker(eng, name):
            count = [0]

            def link(ins):
                count[0] += 1
                ins.then_inc(sem(name), 1)
                eng.wait_ge(sem(name), count[0])
            return link

        @block.sync
        def _(sp):
            def one(dst, src):
                sp.dma_start(dst, src).then_inc(sem("consts_in"), 16)
                consts[0] += 1
            consts = [0]

            def load_x(t):
                if t >= 2:
                    sp.wait_ge(sem("xn_ready"), t - 1)
                src = x_prompt[0, t * P:(t + 1) * P, :] if t < PT else x_sample.rearrange("b t d -> (b t) d")
                sp.dma_start(xb[t % 2][0:rows(t), :], src).then_inc(sem(f"x_in{t % 2}"), 16)

            def load_w(b):
                if b >= 2:
                    sp.wait_ge(sem("proj"), last_of_block[b - 2] + 1)
                c0, n = BLOCKS[b]
                sp.dma_start(wb[b % 2][:, :, 0:n],
                             w_in[0].rearrange("(k p) c -> p k c", p=P)[:, :, c0:c0 + n]).then_inc(sem(f"w_in{b % 2}"), 16)

            load_x(0)
            load_x(1)
            load_w(0)
            with nc.allow_non_contiguous_dma("small vectors, channel on the partition"):
                one(g1, norm1_g[0].rearrange("(k p) -> p k", p=P))
                one(g2n, norm2_g[0].rearrange("(k p) -> p k", p=P))
                one(mu, shift_mu[0].rearrange("(k p) -> p k", p=P))
                one(w0a0[:, 0:HP], w0[0].rearrange("(k p) -> p k", p=P))
                one(w0a0[:, HP:], a0[0].rearrange("(k p) -> p k", p=P))
                one(kkv, k_k[0].rearrange("(k p) -> p k", p=P))
                one(kav[:, 0, :], k_a[0].rearrange("(k p) -> p k", p=P))
                one(rkv, r_k[0].rearrange("(hp h) d -> (h d) hp", h=2))
            one(gq, q_norm_g.partition_broadcast(P).rearrange("p a d -> p (a d)"))
            one(gk, k_norm_g[0].partition_broadcast(P))
            one(gb, gate_b.partition_broadcast(P).rearrange("p a d -> p (a d)"))
            for h in range(2):
                half = slice(64 * h, 64 * h + 64)
                one(lnw[half], lnx_w[0].rearrange("(hp h d) -> h hp d", h=2, d=HD)[h].partition_broadcast(64))
                one(lnb[half], lnx_b[0].rearrange("(hp h d) -> h hp d", h=2, d=HD)[h].partition_broadcast(64))
            one(lora[0:32, :], w2[0])
            one(lora[32:64, :], a2[0])
            one(lora[64:128, :], g2[0])
            one(rope_t, rope.rearrange("t p a b -> p t a b"))
            one(pages[:, :], page_table.rearrange("b n -> (b n)").unsqueeze(0))
            assert consts[0] == CONSTS
            for t in range(2, TILES):
                load_x(t)
            load_w(1)
            sp.wait_ge(sem("xn_turned"), 2 * TILES)
            sp.dma_start(shift_raw[0:DEC_B, :], state_shift[0]).then_inc(sem("shift_in"), 16)
            for b in range(2, len(BLOCKS)):
                load_w(b)
            for t in range(TILES):
                sp.wait_ge(sem("kv_final"), t + 1)
                for br, (pout, sout) in enumerate(((prompt_cmp, sample_cmp), (prompt_slc, sample_slc), (prompt_win, None))):
                    c0 = D_ATTN + 2 * D_KV * br
                    if t < PT and br < 2:
                        dst = pout[0, 0, t].rearrange("p a g d -> p (a g d)")
                    elif t < PT:
                        w = t * P - (SEQ - WINDOW)
                        if w < 0:
                            continue
                        dst = pout[0, 0, w:w + P].rearrange("p a g d -> p (a g d)")
                    elif br < 2:
                        dst = sout[0].rearrange("b t a g d -> (b t) (a g d)")
                    else:
                        for b in range(DEC_B):
                            sp.dma_start(sample_win[0, b, WINDOW - DEC_T:].rearrange("t a g d -> t (a g d)"),
                                         za[b * DEC_T:(b + 1) * DEC_T, t, c0:c0 + 2 * D_KV]).then_inc(sem("stored"), 16)
                            stores[0] += 1
                        continue
                    if t < PT and br == 0:
                        sp.dma_start(dst, za[:, t, c0:c0 + 2 * D_KV]).then_inc(sem("cmp_stored"), 16)
                        continue
                    sp.dma_start(dst, za[0:rows(t), t, c0:c0 + 2 * D_KV]).then_inc(sem("stored"), 16)
                    stores[0] += 1
            sp.dma_start(sample_win[0, :, 0:WINDOW - DEC_T].rearrange("b t a g d -> b (t a g d)"),
                         cache_win_kv[0, :, DEC_T:].rearrange("b t a g d -> b (t a g d)")).then_inc(sem("stored"), 16)
            stores[0] += 1
            sp.wait_ge(*once("shift_out"))
            sp.dma_start(sample_shift[0], shift_rows[0:DEC_B, :]).then_inc(sem("shift_stored"), 16)
            sp.dma_start(prompt_shift[0], shift_rows[DEC_B:DEC_B + 1, :]).then_inc(sem("shift_stored"), 16)
            sp.wait_ge(sem("shift_stored"), 32)
            sp.wait_ge(*once("rw_prompt_done"))
            sp.dma_start(shaped(s0raw[0:64, :, :].rearrange("p b n -> p (b n)"), DEC_B * HEADS, HD),
                         state_wkv[0].rearrange("b h v k -> v (b h) k")).then_inc(sem("s0_in"), 16)
            sp.wait_ge(*once("rw_pstate_rows"))
            sp.dma_start(prompt_wkv[0, 0].rearrange("(hp h) v k -> v hp h k", h=2),
                         st_rows[0:64].rearrange("p a (h k) -> p a h k", h=2)).then_inc(sem("stored"), 16)
            sp.wait_ge(sem("rw_sstate_rows"), DEC_B)
            sp.dma_start(sample_wkv[0].rearrange("b h v k -> v (b h) k"),
                         shaped(sst_rows[0:64].rearrange("p b n -> p (b n)"), DEC_B * HEADS, HD)).then_inc(sem("stored"), 16)
            stores[0] += 2
            sp.wait_ge(sem("stored"), 16 * stores[0])
            sp.wait_ge(*once("rw_all_done"))
            with nc.allow_non_contiguous_dma("256-byte runs of the compression weights"):
                for c in range(2):
                    for i in range(2):
                        sp.dma_start(wcmp[:, c, :, i, :], cmp_w[0, c, i * STRIDE:(i + 1) * STRIDE].rearrange(
                            "(sp s) d e -> (s d) sp e", s=2)).then_inc(sem("wcmp_in"), 16)
                        sp.dma_start(pecol[:, c, i, :], cmp_pe[0, c, i * STRIDE:(i + 1) * STRIDE].rearrange(
                            "(sp s) d -> (s d) sp", s=2)).then_inc(sem("wcmp_in"), 16)
            def page(b, n):
                return sp.value_load(pages[0:1, b * NPG + n:b * NPG + n + 1], min_val=0,
                                     max_val=cache_cmp_kv.shape[1] - 1)

            def load_chunks(u):
                if u >= 2:
                    sp.wait_ge(sem("cm_rows"), u - 1)
                    sp.wait_ge(sem("cm_krows"), u - 1)
                flat = chunk_flat[u % 2]
                if u == 0:
                    sp.dma_start(flat[0:SEQ // STRIDE, :], prompt_cmp[0, 0].rearrange(
                        "n (c s) a g d -> (n c) (s a g d)", s=STRIDE)).then_inc(sem("chunk_in0"), 16)
                    return
                rows_of_page = PAGE // STRIDE
                for n in range(NPG):
                    src = cache_cmp_kv[0, bass.ds(page(u - 1, n), 1)].rearrange("o (c s) a g d -> (o c) (s a g d)", s=STRIDE)
                    sp.dma_start(flat[n * rows_of_page:(n + 1) * rows_of_page, :], src).then_inc(sem(f"chunk_in{u % 2}"), 16)

            sp.wait_ge(sem("cmp_stored"), 16 * PT)
            for u in range(NSEQ):
                load_chunks(u)
            for b in range(DEC_B):
                sp.dma_start(vnew[0:DEC_T, b], shaped(za[b * DEC_T:(b + 1) * DEC_T, PT, D_ATTN + 2 * D_KV:GATE0], 2, 2, D_KV)[:, :, 1, :]).then_inc(sem("vnew_in"), 16)
            for b in range(DEC_B):
                if b == 0:
                    sp.wait_ge(*once("pa_done"))
                else:
                    sp.wait_ge(sem("sa_vcopied"), b)
                if b % 2 == 0 and b > 0:
                    sp.wait_ge(sem("sa_out"), b // 2)
                for n in range(NPG):
                    src = cache_slc_kv[0, bass.ds(page(b, n), 1)].rearrange("o s a g d -> (o s) (a g d)")
                    sp.dma_start(ctok[:, n, :], src).then_inc(sem("ctok_in"), 16)
                sp.dma_start(wtok[:, b % 2], cache_win_kv[0, b].rearrange("(n p) a g d -> p n (a g d)", p=P)).then_inc(sem("wtok_in"), 16)
            sp.wait_ge(*once("att_all_done"))
            sp.dma_start(wo, w_out[0].rearrange("(k p) n -> p k n", p=P)).then_inc(sem("wo_in"), 16)

            def load_x2(t):
                if t >= 2:
                    sp.wait_ge(sem("h_ready"), t - 1)
                src = x_prompt[0, t * P:(t + 1) * P, :] if t < PT else x_sample.rearrange("b t d -> (b t) d")
                sp.dma_start(x2[t % 2][0:rows(t), :], src).then_inc(sem(f"x2_in{t % 2}"), 16)
            load_x2(0)
            load_x2(1)
            sp.dma_start(wdn, w_down[0, 0:GF * P].rearrange("(f p) n -> p f n", p=P)).then_inc(sem("wdn_in"), 16)
            for t in range(2, TILES):
                load_x2(t)
            for g in range(NG):
                if g == 0:
                    sp.wait_ge(sem("h_mm"), TILES)
                else:
                    sp.wait_ge(sem("up"), 3 * GF * g)
                sp.dma_start(wup, w_up[0].rearrange("(k p) n -> p k n", p=P)[:, :, g * GF * P:(g + 1) * GF * P]).then_inc(sem("wup_in"), 16)
                if g > 0:
                    sp.wait_ge(sem("down"), 2 * TILES * g)
                    sp.dma_start(wdn, w_down[0, g * GF * P:(g + 1) * GF * P].rearrange("(f p) n -> p f n", p=P)).then_inc(sem("wdn_in"), 16)
            for t in range(TILES):
                sp.wait_ge(sem("y_sum"), 2 * TILES * (NG - 1) + 2 * t + 2)
                dst = y_prompt[0, t * P:(t + 1) * P, :] if t < PT else y_sample.rearrange("b t d -> (b t) d")
                sp.dma_start(dst, y[0:rows(t), t, :]).then_inc(sem("stored"), 16)
                stores[0] += 1
            sp.wait_ge(sem("stored"), 16 * stores[0])

        @block.gpsimd
        def _(pool):
            link = linker(pool, "pool_chain")

            def select(m, op, base, cm, pattern, fill=0.0):
                link(nc.gpsimd.affine_select(out=m, in_=m, compare_op=op, fill=fill, base=base,
                                             pattern=pattern, channel_multiplier=cm))

            link(nc.gpsimd.memset(ident, 0.0))
            link(nc.gpsimd.affine_select(out=ident, in_=ident, compare_op=ALU.not_equal, fill=1.0, base=0,
                                         pattern=[[-1, P]], channel_multiplier=1))
            link(nc.gpsimd.iota(it_row, pattern=[[0, 1]], base=0, channel_multiplier=1))
            nc.gpsimd.iota(it_col, pattern=[[1, P]], base=0, channel_multiplier=0).then_inc(once("iotas")[0], 1)
            link(nc.gpsimd.memset(num[:, 0:1], 1e-6))
            link(nc.gpsimd.memset(num[:, 1:2], 64e-5))
            nc.gpsimd.memset(rt[:, :, 0:1], 0.0).then_inc(once("ident_ready")[0], 1)
            for h in range(2):
                half = slice(64 * h, 64 * h + 64)
                link(nc.gpsimd.memset(block_ones[half, :], 0.0))
                link(nc.gpsimd.memset(block_ones[half, half], 1.0))
            link(nc.gpsimd.memset(scan_keep, 1.0))
            link(nc.gpsimd.memset(shaped(scan_keep[:, 0, :], HP, CH)[:, :, 0:1], 0.0))
            link(nc.gpsimd.memset(shaped(scan_keep[:, 1, :], HP * DEC_B, DEC_T)[:, :, 0:1], 0.0))
            link(nc.gpsimd.memset(m_a, 1.0))
            link(nc.gpsimd.memset(m_t, 1.0))
            link(nc.gpsimd.memset(m_one, 0.0))
            link(nc.gpsimd.memset(shaped(m_one, CH // 2, 2)[:, :, 0:1], 1.0))
            link(nc.gpsimd.memset(m_onet, 0.0))
            link(nc.gpsimd.memset(shaped(m_onet, CH // 2, 2)[:, :, 1:2], 1.0))
            link(nc.gpsimd.memset(m_lev, 0.0))
            for i, s in enumerate(LEVELS):
                link(nc.gpsimd.memset(shaped(m_lev[:, i, :], CH // (2 * s), 2, s)[:, :, 1, :], 1.0))
            link(nc.gpsimd.memset(row_of, 1.0))

            def same_block(m, size, inner, last):
                nb = CH // size
                pat = [[size, nb]] + [[0, n] for n in inner]
                neg = [[-size, nb]] + [[0, n] for n in inner]
                select(m, ALU.is_ge, 0, 1, neg)
                select(m, ALU.is_ge, last, -1, pat)

            for h in range(2):
                half = slice(64 * h, 64 * h + 64)
                for k in range(2):
                    select(m_a[half, k, :], ALU.is_gt, 0, 1, [[-1, CH]])
                    select(m_t[half, k, 0, :], ALU.is_gt, 0, -1, [[1, CH]])
                    select(m_t[half, k, 1, :], ALU.is_ge, 0, -1, [[1, CH]])
                same_block(shaped(m_a[half, 1, :], DEC_B, DEC_T), DEC_T, [DEC_T], DEC_T - 1)
                for k in range(2):
                    same_block(shaped(m_t[half, 1, k, :], DEC_B, DEC_T), DEC_T, [DEC_T], DEC_T - 1)
                select(shaped(m_one[half, :], CH // 2, 2), ALU.is_equal, -1, 1, [[-2, CH // 2], [0, 2]])
                select(shaped(m_onet[half, :], CH // 2, 2), ALU.is_equal, 0, 1, [[-2, CH // 2], [0, 2]])
                for i, s in enumerate(LEVELS):
                    same_block(shaped(m_lev[half, i, :], CH // (2 * s), 2, s), 2 * s, [2, s], s - 1)
                select(row_of[half, :], ALU.is_ge, 0, 1, [[-DEC_T, DEC_B]])
                select(row_of[half, :], ALU.is_ge, DEC_T - 1, -1, [[DEC_T, DEC_B]])
            link(nc.gpsimd.memset(causal_add, 0.0))
            select(causal_add, ALU.is_ge, 0, 1, [[-1, P]], NEG)
            link(nc.gpsimd.memset(edge_add, 0.0))
            select(edge_add, ALU.is_gt, 0, -1, [[1, P]], NEG)
            link(nc.gpsimd.memset(cmp_keep, 1.0))
            select(cmp_keep, ALU.is_ge, 1 - BLOCK, 1, [[P, PT], [-STRIDE, NCMP_P]])
            link(nc.gpsimd.memset(cmp_add, 0.0))
            select(cmp_add, ALU.is_ge, 1 - BLOCK, 1, [[P, PT], [-STRIDE, NCMP_P]], NEG)
            link(nc.gpsimd.memset(before, 1.0))
            select(before, ALU.is_gt, 0, 0, [[1, NBLK], [-1, NBLK]])
            link(nc.gpsimd.memset(e_scale[:, 0:1], -1.0))
            link(nc.gpsimd.memset(e_scale[:, 1:2], 1.0))
            link(nc.gpsimd.memset(e_scale[:, 2:3], 0.0))
            link(nc.gpsimd.memset(e_scale[0:32, 0:1], -2.0))
            link(nc.gpsimd.memset(e_scale[0:32, 1:2], 2.0))
            nc.gpsimd.memset(e_scale[0:32, 2:3], -1.0).then_inc(once("masks_ready")[0], 1)

            def none(ticks):
                def g(c):
                    for _ in range(ticks):
                        yield
                return g

            def lev_pool(c):
                for i in range(len(LEVELS)):
                    if i < nlev(c):
                        n = lev0(c) + i
                        if i == 0:
                            pool.wait_ge(sem("rw_prod_sb"), c + 1)
                        if n >= 2:
                            pool.wait_ge(sem("rw_x"), min(n - 1, lev0(c) + i - 1))
                        nc.gpsimd.tensor_tensor(amt[:, n % 2], atrb_r[c % 3][:, :, 0, :], spread(m_lev[:, i, :], 1, HP),
                                                ALU.mult).then_inc(sem("rw_amt"), 1)
                    yield
                    yield

            staged(none(TICKS[0]), lev_pool, none(TICKS[2]))
            pool.wait_ge(*once("rw_all_done"))
            link(nc.gpsimd.memset(spread_rows[0:NS], 0.0))
            for p_ in range(DEC_B // 2):
                select(shaped(spread_rows[0:NS, p_], 2, HEADS, DEC_T), ALU.not_equal, -2 * DEC_T * p_, 1,
                       [[-DEC_T, 2], [0, HEADS], [-1, DEC_T]], 1.0)
            nc.gpsimd.engine_nop().then_inc(once("spread_ready")[0], 1)
            for u in range(NSEQ):
                pool.wait_ge(sem(f"chunk_in{u % 2}"), chunk_loads(u))
                if u > 0:
                    pool.wait_ge(sem("cm_turned"), 8 * u)
                nc.gpsimd.tensor_copy(*head_rows(u, 1)).then_inc(sem("cm_rows"), 1)

        @block.scalar
        def _(act):
            link = linker(act, "act_chain")

            def inv_rms(out, ss, n, eps):
                link(nc.scalar.activation(out, ss, ACT.Ln, bias=eps, scale=1.0 / n))
                link(nc.scalar.activation(out, out, ACT.Exp, scale=-0.5))

            def norm_rows(t):
                n = rows(t)
                act.wait_ge(sem(f"x_in{t % 2}"), 16 * (t // 2 + 1))
                if t >= 2:
                    act.wait_ge(sem("xn_turned"), 2 * (t - 1))
                link(nc.scalar.activation(xn[t % 2][0:n], xb[t % 2][0:n], ACT.Square, accum_out=stat[0:n, t:t + 1]))
                inv_rms(stat[0:n, t:t + 1], stat[0:n, t:t + 1], D_MODEL, eps_c[0:n])
                nc.scalar.activation(xn[t % 2][0:n], xb[t % 2][0:n], ACT.Copy,
                                     scale=stat[0:n, t:t + 1]).then_inc(sem("xn_ready"), 1)

            act.wait_ge(*once("ident_ready"))
            for t in range(TILES):
                norm_rows(t)

            def head_norm(t):
                act.wait_ge(sem("head_ss"), t + 1)
                ins = head_rs[0:rows(t), t % 2, :]
                link(nc.scalar.activation(ins, ins, ACT.Ln, bias=eps_c[0:rows(t)], scale=1.0 / HD))
                nc.scalar.activation(ins, ins, ACT.Exp, scale=-0.5).then_inc(sem("head_rs"), 1)

            for i, (b, m, s) in enumerate(PROJ):
                act.wait_ge(sem("proj"), i + 1)
                c0, n = BLOCKS[b]
                if s is None:
                    out, src = za[0:rows(m), m, c0:c0 + n], banks[2 + i % 3][0:rows(m), 0:n]
                    if b == 0:
                        out = out.rearrange("p (h g d) -> p g h d", g=KVH, d=HD)
                        src = src.rearrange("p (g h d) -> p g h d", g=KVH, d=HD)
                else:
                    ch = (c0 - ZA) // P + m
                    a, w = SPANS[s]
                    src = banks[2 + i % 3][:, 0:w]
                    if s < 2:
                        out = rt[:, ch, 1 + a:1 + a + w]
                    else:
                        out, src = zs[:, ch, :, 1:], shaped(src, DEC_B, DEC_T)
                nc.scalar.activation(out, src, ACT.Copy).then_inc(sem("proj_out"), 1)
                if i >= att_done + 3 and (i - att_done - 3) % 4 == 0 and (i - att_done - 3) // 4 < TILES:
                    head_norm((i - att_done - 3) // 4)

            def f_act(c):
                r = c % 3
                yield
                act.wait_ge(sem("rw_xs"), c + 1)
                nc.scalar.activation(ebuf, xs[:, 12, :], ACT.Exp, scale=e_scale[:, 0:1]).then_inc(sem("rw_e"), 1)
                act.wait_ge(sem("rw_kkraw"), c + 1)
                nc.scalar.activation(sqk, kkraw, ACT.Square).then_inc(sem("rw_sqk"), 1)
                yield
                yield
                act.wait_ge(sem("rw_vt"), c + 1)
                nc.scalar.activation(vtok_r[r], shaped(banks[2][:, 0:256], HP, CH), ACT.Copy).then_inc(sem("rw_vsb"), 1)
                yield
                act.wait_ge(sem("rw_u"), c + 1)
                nc.scalar.activation(sig, sig, ACT.Exp, scale=-1.0).then_inc(sem("rw_esig"), 1)
                nc.scalar.activation(gtok_r[r], shaped(banks[1][:, 256:512], HP, CH), ACT.Copy).then_inc(sem("rw_gsb"), 1)
                act.wait_ge(sem("rw_ssm"), c + 1)
                link(nc.scalar.activation(ssm, ssm, ACT.Ln, scale=2.0 ** 30))
                nc.scalar.activation(ssm, ssm, ACT.Exp, scale=-0.5).then_inc(sem("rw_rs"), 1)
                yield
                yield
                act.wait_ge(sem("rw_cs"), c + 1)
                nc.scalar.activation(dprev, cx, ACT.Exp, scale=-KAPPA)
                nc.scalar.activation(dinv, cs, ACT.Exp, scale=KAPPA)
                nc.scalar.activation(dec_r[r], cs, ACT.Exp, scale=-KAPPA).then_inc(sem("rw_dec"), 1)
                for _ in range(8):
                    yield
                act.wait_ge(sem("rw_tok"), c + 1)
                nc.scalar.activation(tokbk_r[r].rearrange("p a b c -> p (a b c)"), banks[0], ACT.Copy).then_inc(sem("rw_toksb"), 1)
                yield
                yield

            def l_act(c):
                for i in range(len(LEVELS)):
                    if i < nlev(c):
                        act.wait_ge(sem("rw_x"), lev0(c) + i + 1)
                        nc.scalar.activation(xsb, shaped(banks[3][:, 0:256], HP, CH), ACT.Copy).then_inc(sem("rw_xsb"), 1)
                    yield
                    yield

            def y_act(c):
                if c == NCH:
                    act.wait_ge(*once("rw_pstate"))
                    nc.scalar.activation(st_rows[0:64], shaped(banks[7][0:64, :], HP, P), ACT.Copy).then_inc(once("rw_pstate_rows")[0], 1)
                    for b in range(DEC_B):
                        act.wait_ge(sem("s0_turned"), b + 1)
                        nc.scalar.activation(sst[:, :, b, :], shaped(banks[b % 2][:, 0:256], HP, HD),
                                             ACT.Copy).then_inc(sem("s0_ready"), 1)
                    act.wait_ge(sem("rw_ps"), 1)
                    nc.scalar.activation(pst.rearrange("p a b c -> p (a b c)"), banks[3], ACT.Copy).then_inc(sem("rw_pssb"), 1)
                act.wait_ge(sem("rw_w"), c + 1)
                nc.scalar.activation(wsb, shaped(banks[5][:, 0:256], HP, CH), ACT.Copy).then_inc(sem("rw_wsb"), 1)
                yield
                yield
                yield
                act.wait_ge(sem("rw_var"), c + 1)
                link(nc.scalar.activation(ystat[:, 1, :], ystat[:, 1, :], ACT.Ln, bias=gneps_c, scale=1.0 / HD))
                nc.scalar.activation(ystat[:, 1, :], ystat[:, 1, :], ACT.Exp, scale=-0.5).then_inc(sem("rw_yrs"), 1)
                yield
                yield
                act.wait_ge(sem("rw_yt"), c + 1)
                src = shaped(banks[7][0:64, :], HP, 2, CH)
                for h in range(2):
                    ins = nc.scalar.activation(mixed[HALVES[h], HP:, CH * c:CH * c + CH], src[:, :, h, :], ACT.Copy)
                ins.then_inc(sem("rw_mixed"), 1)
                yield

            staged(f_act, l_act, y_act)
            for b in range(DEC_B):
                act.wait_ge(sem("rw_sstate"), b + 1)
                nc.scalar.activation(sst_rows[0:64, b, :], banks[b % 2][0:64, :], ACT.Copy).then_inc(sem("rw_sstate_rows"), 1)
            act.wait_ge(sem("rw_st"), NCH + 1)
            act.wait_ge(*once("rw_all_done"))
            nc.scalar.activation(gates[:, 0:PT, :], za[:, 0:PT, GATE0:], ACT.Exp, scale=-1.0)
            nc.scalar.activation(gates[0:NS, PT, :], za[0:NS, PT, GATE0:], ACT.Exp, scale=-1.0).then_inc(once("egates")[0], 1)
            for f in range(5):
                act.wait_ge(sem("kt_turned"), f + 1)
                dst = ktp[:, f // 2, 512 * (f % 2):512 * (f % 2) + 512] if f < 4 else ktp[:, :, SEQ:]
                src = banks[f % 4] if f < 4 else shaped(banks[4][:, 0:2 * NS], 2, NS)
                nc.scalar.activation(dst, src, ACT.Copy).then_inc(sem("kt_ready"), 1)
            for u in range(NSEQ):
                for f in range(1, 8, 2):
                    g = 8 * u + f
                    act.wait_ge(sem("cm_turned"), g + 1)
                    if g >= 4:
                        act.wait_ge(sem("cm_mm"), g - 3)
                    n = SEQ // STRIDE if u == 0 else P
                    nc.scalar.activation(xt[g % 4][:, :, :, 0:n], shaped(banks[g % 4], 2, KVH, P)[:, :, :, 0:n],
                                         ACT.Copy).then_inc(sem("cm_x1"), 1)
                ncm = NCMP_P if u == 0 else NCMP
                act.wait_ge(sem("cm_sel"), u + 1)
                nc.scalar.activation(kc_all[:, u, 0:ncm], banks[6][:, 0:ncm], ACT.Copy)
                nc.scalar.activation(vc_all[0:ncm, u], shaped(banks[7][0:ncm, 0:P], KVH, HD), ACT.Copy).then_inc(sem("cm_kv"), 1)

            def empty_turn(e):
                f = turn_no[e]
                if f % 2:
                    act.wait_ge(sem("turn_in"), f + 1)
                    turn_copy(e, act, lambda out, in_, scale: nc.scalar.activation(out, in_, ACT.Copy, scale=scale)).then_inc(sem("turn_out1"), 1)

            for e in events:
                if e[0] in "qTm":
                    empty_turn(e)
                elif e[0] == "S":
                    u = e[1]
                    i, kind, h = units[u]
                    act.wait_ge(sem("pa_max"), u + 1)
                    if u >= 2:
                        act.wait_ge(sem("pa_t"), u - 1)
                    if kind == "c":
                        p = pbuf[u % 2][:, 0:HEADS * NCMP_P]
                        nc.scalar.activation(p, p, ACT.Exp).then_inc(sem("pa_p"), 1)
                    else:
                        n = P * len(key_tiles(u))
                        s0 = 1024 * (u % 2)
                        nc.scalar.activation(pbuf[u % 2][:, 0:n], psum[:, s0:s0 + n], ACT.Exp, bias=pmax[:, u % 4:u % 4 + 1],
                                             accum_out=psum_[:, u % 4:u % 4 + 1]).then_inc(sem("pa_p"), 1)
            act.wait_ge(*once("sq_turned"))
            nc.scalar.activation(qs.rearrange("p b h q -> p h b q"), shaped(banks[0][:, 0:HG * NS], HG, DEC_B, DEC_T),
                                 ACT.Copy, scale=HD ** -0.5).then_inc(once("sq_ready")[0], 1)
            for p_ in range(DEC_B // 2):
                act.wait_ge(sem("sc_max"), p_ + 1)
                nc.scalar.activation(pcs[:, 1:1 + NCMP], banks[0][:, 0:NCMP], ACT.Exp, bias=sst4[:, 0:1],
                                     accum_out=sst4[:, 1:2]).then_inc(sem("sc_p"), 1)
                for bb in range(2):
                    b = 2 * p_ + bb
                    for q in range(4):
                        act.wait_ge(sem("sk_turned"), 4 * b + q + 1)
                        nc.scalar.activation(ktb[:, 512 * q:512 * q + 512], banks[5 + q % 2], ACT.Copy).then_inc(sem("sk_ready"), 1)
                act.wait_ge(sem("ss_max"), p_ + 1)
                nc.scalar.activation(ssel, ssel, ACT.Exp, bias=sst4[:, 0:1], accum_out=sst4[:, 2:3]).then_inc(sem("ss_p"), 1)
                for q in range(1, 4, 2):
                    act.wait_ge(sem("sp_turned"), 6 * p_ + q + 1)
                    nc.scalar.activation(ktb[:, 512 * q:512 * q + 512], banks[q % 4], ACT.Copy).then_inc(sem("sp_act"), 1)
                act.wait_ge(sem("sw_max"), p_ + 1)
                nc.scalar.activation(swin, swin, ACT.Exp, bias=sst4[:, 0:1], accum_out=sst4[:, 3:4]).then_inc(sem("sw_p"), 1)
                act.wait_ge(sem("sp_turned"), 6 * p_ + 6)
                act.wait_ge(sem("sa_os"), p_ + 1)
                link(nc.scalar.activation(ktb[:, 0:512], banks[5], ACT.Copy))
                nc.scalar.activation(ptn[0:DEC_T, 1, :], banks[6][0:DEC_T, 0:P], ACT.Copy).then_inc(sem("sw_pt"), 1)
            act.wait_ge(*once("so_turned"))
            src = banks[0][0:HD, :].rearrange("p (b k h q) -> p b k h q", b=DEC_B, k=HP, h=2)
            for h in range(2):
                ins = nc.scalar.activation(mixed[HALVES[h], 0:HP, SEQ:].rearrange("p k (b q) -> p b k q", q=DEC_T),
                                           src[:, :, :, h, :], ACT.Copy)
            ins.then_inc(once("att_all_done")[0], 1)
            for t in range(TILES):
                n = rows(t)
                act.wait_ge(sem("h_ready"), t + 1)
                if t >= 1:
                    act.wait_ge(sem("h_turned"), 2 * t)
                link(nc.scalar.activation(hn[0:n], y[0:n, t, :], ACT.Square, accum_out=stat[0:n, t:t + 1]))
                inv_rms(stat[0:n, t:t + 1], stat[0:n, t:t + 1], D_MODEL, eps_c[0:n])
                nc.scalar.activation(hn[0:n], y[0:n, t, :], ACT.Copy, scale=stat[0:n, t:t + 1]).then_inc(sem("hn_ready"), 1)
            for g in range(NG):
                for j in range(3 * GF):
                    f, s = divmod(j, 3)
                    n = 3 * GF * g + j
                    act.wait_ge(sem("up"), n + 1)
                    if g > 0 and j == 0:
                        act.wait_ge(sem("down"), 2 * TILES * g)
                    nc.scalar.activation(act_of(f, s), banks[n % 4][:, 0:SPANS[s][1]], ACT.Relu).then_inc(sem("relu"), 1)

        @block.tensor
        def _(pe):
            def mm(out, lhsT, rhs, start=True, stop=True):
                return nc.tensor.matmul(out, lhsT, rhs, start=start, stop=stop)

            pe.wait_ge(*once("ident_ready"))
            for t in range(TILES):
                n = rows(t)
                pe.wait_ge(sem("xn_ready"), t + 1)
                for half in range(2):
                    if t >= 1:
                        pe.wait_ge(sem("nt_out"), 2 * t + half - 1)
                    for k in range(4):
                        c = 4 * half + k
                        ins = nc.tensor.transpose(banks[half][:, k * P:k * P + n],
                                                  xn[t % 2][0:n, c * P:(c + 1) * P], ident[0:n, 0:n])
                    ins.then_inc(sem("xn_turned"), 1)
            pe.wait_ge(sem("nt_out"), 2 * TILES)
            for i, (b, m, s) in enumerate(PROJ):
                if i == 0 or PROJ[i - 1][0] != b:
                    pe.wait_ge(sem(f"w_in{b % 2}"), 16 * (b // 2 + 1))
                if i >= 3:
                    pe.wait_ge(sem("proj_out"), i - 2)
                c0, n = BLOCKS[b]
                for k in range(KT):
                    if s is None:
                        ins = mm(banks[2 + i % 3][0:rows(m), 0:n], nt[:, k, m * P:m * P + rows(m)],
                                 wb[b % 2][:, k, 0:n], k == 0, k == KT - 1)
                    else:
                        a, w = SPANS[s]
                        ins = mm(banks[2 + i % 3][:, 0:w], wb[b % 2][:, k, m * P:(m + 1) * P],
                                 nt[:, k, a:a + w], k == 0, k == KT - 1)
                ins.then_inc(sem("proj"), 1)
            pe.wait_ge(sem("shift_in"), 16)
            for c in range(RC):
                ins = nc.tensor.transpose(banks[0][:, c * DEC_B:(c + 1) * DEC_B],
                                          shift_raw[0:DEC_B, c * P:(c + 1) * P], ident[0:DEC_B, 0:DEC_B])
            ins.then_inc(once("shift_turned")[0], 1)
            pe.wait_ge(*once("last_cols"))
            for c in range(RC):
                ins = nc.tensor.transpose(banks[4 + c // 4][0:DEC_B + 1, (c % 4) * P:(c % 4 + 1) * P],
                                          last_cols[:, c, :], ident)
            ins.then_inc(once("last_turned")[0], 1)

            def f_pe(c):
                r = c % 3
                yield
                yield
                yield
                pe.wait_ge(sem("rw_xs"), c + 1)
                for hp in range(HP):
                    for h in HALVES:
                        ins = mm(banks[2][h, hp * CH:(hp + 1) * CH], xs[h, 8 + hp, :], ident[h, h])
                ins.then_inc(sem("rw_vt"), 1)
                pe.wait_ge(sem("rw_l"), c + 1)
                if c > 0:
                    pe.wait_ge(sem("rw_toksb"), c)
                for q in range(2):
                    for hp in range(HP):
                        mm(banks[q][:, hp * CH:(hp + 1) * CH],
                           lora[32 * q:32 * q + 32, hp * P:(hp + 1) * P], lbuf[32 * q:32 * q + 32, :])
                pe.wait_ge(sem("rw_sqk"), c + 1)
                mm(banks[0][:, 256:512], block_ones, sqk.rearrange("p a b -> p (a b)"))
                for i, h in enumerate(HALVES):
                    ins = mm(shaped(banks[1][h, 256:512], HP, CH), lbuf[64:128, :],
                             shaped(lora[64:128, :], HP, 2, HD)[:, :, i, :])
                ins.then_inc(sem("rw_wa"), 1)
                for _ in range(8):
                    yield
                pe.wait_ge(sem("rw_prbk"), c + 1)
                pe.wait_ge(sem("rw_gsb"), c + 1)
                pe.wait_ge(sem("rw_vsb"), c + 1)
                pr = pr_r[r]
                for hp in range(HP):
                    for h in HALVES:
                        both = pr[h, hp, :, :].rearrange("p a b -> p (a b)")
                        mm(banks[0][h, hp * P:(hp + 1) * P], bk[h, hp, 0, :], both)
                        mm(banks[1][h, hp * P:(hp + 1) * P], bk[h, hp, 1, :], both)
                        mm(banks[2][h, 256 + hp:257 + hp], rkk[h, hp, :], block_ones[h, h][:, 0:1])
                        ins = mm(banks[2][h, hp * CH:(hp + 1) * CH], pr[h, hp, 0, :], bk[h, hp, 0, :])
                    if hp == 1:
                        yield
                ins.then_inc(sem("rw_prod"), 1)
                yield
                pe.wait_ge(sem("rw_prod_sb"), c + 1)
                for hp in range(HP):
                    for h in HALVES:
                        for q in range(2):
                            ins = mm(banks[0][h, (q * HP + hp) * CH:(q * HP + hp + 1) * CH], bk[h, hp, q, :], ident[h, h])
                ins.then_inc(sem("rw_tok"), 1)
                yield
                yield
                yield

            def l_pe(c):
                tu = tu_r[c % 3]
                for i in range(len(LEVELS)):
                    if i >= nlev(c):
                        yield
                        yield
                        continue
                    n = lev0(c) + i
                    pe.wait_ge(sem("rw_amt"), n + 1)
                    if i == 0:
                        pe.wait_ge(sem("rw_ti"), c + 1)
                    if n > 0:
                        pe.wait_ge(sem("rw_t"), n)
                    for hp in range(HP):
                        for h in HALVES:
                            ins = mm(banks[3][h, hp * CH:(hp + 1) * CH], amt[h, n % 2, hp, :], tu[h, hp, 0, :])
                    ins.then_inc(sem("rw_x"), 1)
                    yield
                    pe.wait_ge(sem("rw_xsb"), n + 1)
                    for hp in range(HP):
                        for h in HALVES:
                            if i < nlev(c) - 1:
                                mm(banks[4][h, hp * P:hp * P + CH], tu[h, hp, 1, :], xsb[h, hp, :])
                            ins = mm(banks[4][h, hp * P + CH:(hp + 1) * P], xsb[h, hp, :], tu[h, hp, 1, :])
                    ins.then_inc(sem("rw_tx"), 1)
                    yield

            def y_pe(c):
                r = c % 3
                pr, tu, atrb, gtrk, tokbk, vtok = (x[r] for x in (pr_r, tu_r, atrb_r, gtrk_r, tokbk_r, vtok_r))
                if c == NCH:
                    pe.wait_ge(sem("rw_st"), NCH)
                    pe.wait_ge(sem("rw_mixed"), NCH)
                    for hp in range(HP):
                        ins = nc.tensor.transpose(banks[7][0:64, hp * P:(hp + 1) * P], st[:, hp, :], ident)
                    ins.then_inc(once("rw_pstate")[0], 1)
                    pe.wait_ge(sem("s0_in"), 16)
                    pe.wait_ge(sem("rw_toksb"), NCH + 1)
                    for b in range(DEC_B):
                        if b >= 2:
                            pe.wait_ge(sem("s0_ready"), b - 1)
                        for hp in range(HP):
                            ins = nc.tensor.transpose(banks[b % 2][:, hp * HD:(hp + 1) * HD],
                                                      s0raw[0:64, b, hp * P:(hp + 1) * P], ident[0:64, 0:64])
                        ins.then_inc(sem("s0_turned"), 1)
                    pe.wait_ge(sem("s0_ready"), DEC_B)
                    for b in range(DEC_B):
                        for hp in range(HP):
                            for h in HALVES:
                                ins = mm(shaped(banks[3][h, hp * P:(hp + 1) * P], 2, DEC_B, DEC_T)[:, :, b, :], sst[h, hp, b, :],
                                         pr[h, hp, :, b * DEC_T:(b + 1) * DEC_T])
                    ins.then_inc(sem("rw_ps"), 1)
                    pe.wait_ge(sem("rw_pssb"), 1)
                elif c > 0:
                    pe.wait_ge(sem("rw_st"), c)
                else:
                    pe.wait_ge(*once("rw_st0"))
                for hp in range(HP):
                    for h in HALVES:
                        out = banks[5][h, hp * CH:(hp + 1) * CH]
                        if c < NCH:
                            mm(out, pr[h, hp, 0, :], st[h, hp, :], True, False)
                        else:
                            mm(out, pst[h, hp, 0, :], ident[h, h], True, False)
                        ins = mm(out, gtrk[h, hp, 0, :], vtok[h, hp, :], False, True)
                ins.then_inc(sem("rw_w"), 1)
                yield
                pe.wait_ge(sem("rw_wsb"), c + 1)
                pe.wait_ge(sem("rw_t"), lev0(c) + nlev(c))
                pe.wait_ge(sem("rw_toksb"), c + 1)
                for hp in range(HP):
                    for h in HALVES:
                        ins = mm(banks[5][h, 256 + hp * CH:256 + (hp + 1) * CH], tu[h, hp, 1, :], wsb[h, hp, :])
                ins.then_inc(sem("rw_uu"), 1)
                yield
                pe.wait_ge(sem("rw_nu"), c + 1)
                if c < NCH:
                    for hp in range(HP):
                        for h in HALVES:
                            out = banks[6][h, hp * CH:(hp + 1) * CH]
                            mm(out, tokbk[h, 0, hp, :], nu[h, hp, :], True, False)
                            ins = mm(out, tokbk[h, 1, hp, :], vtok[h, hp, :], False, True)
                else:
                    for hp, q in enumerate(SBANK):
                        for h in HALVES:
                            mm(banks[q][h, :], tokbk[h, 0, hp, :], nub[h, hp, :, :].rearrange("p a b -> p (a b)"), True, False)
                            ins = mm(banks[q][h, :], tokbk[h, 1, hp, :], vb[h, hp, :, :].rearrange("p a b -> p (a b)"), False, True)
                for hp in range(HP):
                    for h in HALVES:
                        out = banks[6][h, 256 + hp * CH:256 + (hp + 1) * CH]
                        if c < NCH:
                            mm(out, pr[h, hp, 1, :], st[h, hp, :], True, False)
                        else:
                            mm(out, pst[h, hp, 1, :], ident[h, h], True, False)
                        mm(out, atrb[h, hp, 1, :], nu[h, hp, :], False, False)
                        ins = mm(out, gtrk[h, hp, 1, :], vtok[h, hp, :], False, True)
                ins.then_inc(sem("rw_y"), 1)
                yield
                yield
                yield
                pe.wait_ge(sem("rw_yo"), c + 1)
                if c > 0:
                    pe.wait_ge(sem("rw_mixed"), c)
                if c == NCH:
                    pe.wait_ge(*once("rw_pstate_rows"))
                for hp in range(HP):
                    ins = nc.tensor.transpose(banks[7][0:64, hp * P:(hp + 1) * P], yc[:, hp, :], ident)
                ins.then_inc(sem("rw_yt"), 1)
                yield

            staged(f_pe, l_pe, y_pe)
            pe.wait_ge(sem("rw_st"), NCH + 1)
            for b in range(DEC_B):
                if b >= 2:
                    pe.wait_ge(sem("rw_sstate_rows"), b - 1)
                for hp in range(HP):
                    ins = nc.tensor.transpose(banks[b % 2][0:64, hp * P:(hp + 1) * P], sst[:, hp, b, :], ident)
                ins.then_inc(sem("rw_sstate"), 1)
            pe.wait_ge(sem("kv_final"), TILES)
            pe.wait_ge(sem("rw_sstate_rows"), DEC_B)
            for f in range(5):
                if f < 4:
                    br = 1 + f // 2
                    c0 = D_ATTN + 2 * D_KV * br
                    for q in range(4):
                        t = 4 * (f % 2) + q
                        ins = nc.tensor.transpose(banks[f][:, q * P:(q + 1) * P], za[:, t, c0:c0 + D_KV], ident)
                else:
                    for br in (1, 2):
                        c0 = D_ATTN + 2 * D_KV * br
                        ins = nc.tensor.transpose(banks[4][:, (br - 1) * NS:br * NS], za[0:NS, PT, c0:c0 + D_KV], ident[0:NS, 0:NS])
                ins.then_inc(sem("kt_turned"), 1)
            pe.wait_ge(sem("wcmp_in"), 16 * 8)
            pe.wait_ge(sem("kt_ready"), 5)
            for c in range(2):
                for sp_ in range(STRIDE // 2):
                    ins = mm(banks[5][:, 2 * c:2 * c + 2], wcmp[:, c, sp_].rearrange("p a b -> p (a b)"), pecol[:, c, :, sp_],
                             sp_ == 0, sp_ == STRIDE // 2 - 1)
            ins.then_inc(once("pe_sum")[0], 1)
            pe.wait_ge(*once("pe_bias"))

            def cm_products(g):
                u, f = divmod(g, 8)
                n = SEQ // STRIDE if u == 0 else P
                pe.wait_ge(sem(f"cm_x{g % 2}"), g // 2 + 1)
                if f == 0 and u > 0:
                    pe.wait_ge(sem("cm_y"), u)
                for j in range(2):
                    k = 2 * f + j
                    c, sp_ = divmod(k, STRIDE // 2)
                    ins = mm(shaped(banks[4 + c][:, 0:KVH * n], KVH, n), wcmp[:, c, sp_].rearrange("p a b -> p (a b)"),
                             xt[g % 4][:, j, :, 0:n], sp_ == 0, sp_ == STRIDE // 2 - 1)
                ins.then_inc(sem("cm_mm"), 1)

            def cm_select(u):
                n = NCMP_P if u == 0 else NCMP
                pe.wait_ge(sem("cm_y"), u + 1)
                if u > 0:
                    pe.wait_ge(sem("cm_kv"), u)
                for g in range(KVH):
                    for i in range(2):
                        mm(banks[6][HALVES[g], 0:n], ident[:, HD * i:HD * i + HD], ycmp[:, 0, g, i:i + n], i == 0, i == 1)
                for g in range(KVH):
                    for i in range(2):
                        ins = mm(banks[7][0:n, HD * g:HD * g + HD], ycmp[:, 1, g, i:i + n], ident[:, HD * i:HD * i + HD], i == 0, i == 1)
                ins.then_inc(sem("cm_sel"), 1)

            for g in range(8 * NSEQ + 3):
                if g < 8 * NSEQ:
                    u, f = divmod(g, 8)
                    n = SEQ // STRIDE if u == 0 else P
                    if f == 0:
                        pe.wait_ge(sem("cm_krows"), u + 1)
                    if f == 4:
                        pe.wait_ge(sem("cm_rows"), u + 1)
                    for j in range(2):
                        c, sp_ = divmod(2 * f + j, STRIDE // 2)
                        for kv in range(KVH):
                            ins = nc.tensor.transpose(shaped(banks[g % 4], 2, KVH, P)[:, j, kv, 0:n],
                                                      by_head[0:n, 2 * c + kv, 2 * sp_:2 * sp_ + 2, :].rearrange("p a b -> p (a b)"), ident[0:n, 0:n])
                    ins.then_inc(sem("cm_turned"), 1)
                if g >= 2 and g - 2 < 8 * NSEQ:
                    cm_products(g - 2)
                    if (g - 2) % 8 == 7:
                        cm_select((g - 2) // 8)
            pe.wait_ge(sem("cm_kv"), NSEQ)
            pe.wait_ge(*once("q_zero"))

            def turn_wait(e):
                f = turn_no[e]
                if f >= 2:
                    pe.wait_ge(sem(f"turn_out{f % 2}"), f // 2)
                return banks[4 + f % 2]

            for e in events:
                if e[0] == "q":
                    b = turn_wait(e)
                    for hh in range(HG):
                        ins = nc.tensor.transpose(b[:, hh * P:(hh + 1) * P],
                                                  za[:, e[1], hh * P:(hh + 1) * P], ident)
                    ins.then_inc(sem("turn_in"), 1)
                elif e[0] == "S":
                    u = e[1]
                    i, kind, h = units[u]
                    if kind == "c":
                        f = turn_no[("q", i)]
                        pe.wait_ge(sem(f"turn_out{f % 2}"), f // 2 + 1)
                    if u >= 2:
                        pe.wait_ge(sem("pa_p"), u - 1)
                    s0 = 1024 * (u % 2)
                    if kind == "c":
                        for h in range(HEADS):
                            c0 = s0 + 512 * (h // HG) + h % HG * NCMP_P
                            ins = mm(psum[:, c0:c0 + NCMP_P], qt[i % 2][:, h // HG, h % HG, :], kc_all[:, 0, 0:NCMP_P])
                    else:
                        ks = key_tiles(u)
                        for j in range(0, len(ks), 4):
                            n = min(4, len(ks) - j) * P
                            k0 = ks[j] * P
                            ins = mm(psum[:, s0 + j * P:s0 + j * P + n], qt[i % 2][:, h // HG, h % HG, :], ktp[:, int(kind == "w"), k0:k0 + n])
                    ins.then_inc(sem("pa_s"), 1)
                elif e[0] == "T":
                    _, u, j = e
                    b = turn_wait(e)
                    if j == 0:
                        pe.wait_ge(sem("pa_pm" if units[u][1] == "c" else "pa_p"), (units[u][0] if units[u][1] == "c" else u) + 1)
                    ks = parts_of(u)
                    for q in range(len(ks[j])):
                        if units[u][1] == "c":
                            h = ks[j][q]
                            ins = nc.tensor.transpose(b[0:NCMP_P, q * P:(q + 1) * P], pbuf[u % 2][:, h * NCMP_P:(h + 1) * NCMP_P], ident)
                        else:
                            k = 4 * j + q
                            ins = nc.tensor.transpose(b[:, q * P:(q + 1) * P], pbuf[u % 2][:, k * P:(k + 1) * P], ident)
                    ins.then_inc(sem("turn_in"), 1)
                    if j == len(ks) - 1:
                        pe.wait_ge(sem("turn_in"), turn_no[e] + 1)
                        pe.sem_inc(sem("pa_t"), 1)
                elif e[0] == "O":
                    u = e[1]
                    i, kind, h = units[u]
                    ps = parts_of(u)
                    for j in range(len(ps)):
                        f = turn_no[("T", u, j)]
                        pe.wait_ge(sem(f"turn_out{f % 2}"), f // 2 + 1)
                    if u >= 2:
                        pe.wait_ge(sem("pa_acc"), u - 1)
                    b = banks[6 + u % 2]
                    total = sum(len(x) for x in ps)
                    k = 0
                    for j in range(len(ps)):
                        s = slot_no[("T", u, j)]
                        for q in range(len(ps[j])):
                            w = ptb[s % 4][:, q * P:(q + 1) * P]
                            if kind == "c":
                                hh = ps[j][q]
                                ins = mm(b[:, hh * HD:(hh + 1) * HD], w[0:NCMP_P], vc_all[0:NCMP_P, 0, hh // HG, :])
                            else:
                                ins = mm(b[:, 0:HD], w, za[:, ps[j][q], vcols(2 if kind == "w" else 1, h // HG)],
                                         k == 0, k == total - 1)
                            k += 1
                    ins.then_inc(sem("pa_o"), 1)
                else:
                    i = e[1]
                    b = turn_wait(e)
                    pe.wait_ge(sem("pa_acc"), UPT * (i + 1))
                    for c in range(HP):
                        ins = nc.tensor.transpose(b[:, c * P:(c + 1) * P],
                                                  oacc[i % 2].rearrange("p h d -> p (h d)")[:, c * P:(c + 1) * P], ident)
                    ins.then_inc(sem("turn_in"), 1)
            nturn = len(turns)
            pe.wait_ge(sem("turn_out0"), (nturn + 1) // 2)
            pe.wait_ge(sem("turn_out1"), nturn // 2)
            pe.wait_ge(*once("pa_done"))
            for hh in range(HG):
                ins = nc.tensor.transpose(banks[0][:, hh * NS:(hh + 1) * NS],
                                          za[0:NS, PT, hh * P:(hh + 1) * P], ident[0:NS, 0:NS])
            ins.then_inc(once("sq_turned")[0], 1)
            pe.wait_ge(*once("spread_ready"))
            for p_ in range(DEC_B // 2):
                ins = mm(banks[1][:, p_ * P:p_ * P + 3 * HEADS], spread_rows[0:NS, p_, :], gates[0:NS, PT, :])
            ins.then_inc(once("gs_spread")[0], 1)
            pe.wait_ge(*once("sq_ready"))
            pe.wait_ge(sem("vnew_in"), 16 * DEC_B)

            def sq_of(b, g):
                return qs[HALVES[g], b].rearrange("p h q -> p (h q)")

            for p_ in range(DEC_B // 2):
                quads = [(2 * p_ + bb, g, slice(64 * bb + 32 * g, 64 * bb + 32 * g + 32)) for bb in range(2) for g in range(KVH)]
                if p_ > 0:
                    pe.wait_ge(sem("sa_out"), p_)
                for b, g, r in quads:
                    ins = mm(banks[0][r, 0:NCMP], sq_of(b, g), kc_all[HALVES[g], 1 + b, 0:NCMP])
                ins.then_inc(sem("sc_s"), 1)
                for bb in range(2):
                    b = 2 * p_ + bb
                    pe.wait_ge(sem("ctok_in"), 16 * NPG * (b + 1))
                    if bb == 0:
                        pe.wait_ge(sem("sc_pn"), p_ + 1)
                        mm(banks[7][:, 0:NCMP], head_sum, pcs[:, 1:1 + NCMP]).then_inc(sem("sc_hs"), 1)
                        nc.tensor.transpose(banks[4][0:NCMP, 0:P], pcs[:, 1:1 + NCMP], ident).then_inc(sem("sc_t"), 1)
                    for q in range(4):
                        if 4 * b + q >= 2:
                            pe.wait_ge(sem("sk_ready"), 4 * b + q - 1)
                        for n in range(4):
                            ins = nc.tensor.transpose(banks[5 + q % 2][:, n * P:(n + 1) * P], ctok[:, 4 * q + n, 0:D_KV], ident)
                        ins.then_inc(sem("sk_turned"), 1)
                    pe.wait_ge(sem("sk_ready"), 4 * b + 4)
                    if bb == 0:
                        pe.wait_ge(sem("sc_ptr"), p_ + 1)
                    for q in range(4):
                        for b_, g, r in quads[2 * bb:2 * bb + 2]:
                            mm(banks[q][r, :], sq_of(b_, g), ktb[HALVES[g], 512 * q:512 * q + 512])
                    for b_, g, r in quads[2 * bb:2 * bb + 2]:
                        ins = mm(banks[4][r, 0:DEC_T], sq_of(b_, g), ktp[HALVES[g], 0, SEQ + b_ * DEC_T:SEQ + (b_ + 1) * DEC_T])
                    ins.then_inc(sem("ss_s"), 1)
                for b, g, r in quads:
                    ins = mm(banks[7][r, 0:HD], ptn_c[0:NCMP, r], vc_all[0:NCMP, 1 + b, g, :])
                ins.then_inc(sem("sa_oc"), 1)
                pe.wait_ge(sem("ss_p"), p_ + 1)
                for q in range(4):
                    for n in range(4):
                        k = 4 * q + n
                        ins = nc.tensor.transpose(banks[q][:, n * P:(n + 1) * P], ssel[:, k * P:(k + 1) * P], ident)
                    ins.then_inc(sem("sp_turned"), 1)
                nc.tensor.transpose(banks[4][0:DEC_T, 0:P], ssel[:, PAST:], ident).then_inc(sem("sp_turned"), 1)
                pe.wait_ge(sem("wtok_in"), 16 * (2 * p_ + 2))
                for bb in range(2):
                    for n in range(4):
                        ins = nc.tensor.transpose(banks[5 + bb][:, n * P:(n + 1) * P], wtok[:, bb, n, 0:D_KV], ident)
                ins.then_inc(sem("swk_turned"), 1)
                pe.wait_ge(sem("swk_ready"), p_ + 1)
                pe.wait_ge(sem("sa_acc_c"), p_ + 1)
                for b, g, r in quads:
                    mm(banks[7][r, :], sq_of(b, g), swk[b % 2][HALVES[g], :])
                pe.wait_ge(sem("sp_ptn"), p_ + 1)
                for b, g, r in quads:
                    ins = mm(banks[4][r, 0:DEC_T], sq_of(b, g), ktp[HALVES[g], 1, SEQ + b * DEC_T:SEQ + (b + 1) * DEC_T])
                ins.then_inc(sem("sw_s"), 1)
                pe.wait_ge(sem("sp_act"), 2 * p_ + 2)
                pe.wait_ge(sem("sp_dve"), 2 * p_ + 2)
                for b, g, r in quads:
                    for k in range(NPG):
                        mm(banks[0][r, 0:HD], ktb[:, k * P:(k + 1) * P][:, r], vtok2[:, b % 2, k, HD * g:HD * g + HD], k == 0, False)
                    ins = mm(banks[0][r, 0:HD], ptn[0:DEC_T, 0, r], vnew[0:DEC_T, b, 0, HD * g:HD * g + HD], False, True)
                ins.then_inc(sem("sa_os"), 1)
                pe.wait_ge(sem("sw_p"), p_ + 1)
                for n in range(4):
                    nc.tensor.transpose(banks[5][:, n * P:(n + 1) * P], swin[:, n * P:(n + 1) * P], ident)
                nc.tensor.transpose(banks[6][0:DEC_T, 0:P], swin[:, WINDOW:], ident).then_inc(sem("sp_turned"), 1)
                pe.wait_ge(sem("sw_pt"), p_ + 1)
                for b, g, r in quads:
                    for k in range(4):
                        mm(banks[1][r, 0:HD], ktb[:, k * P:(k + 1) * P][:, r], wtok[:, b % 2, k, D_KV + HD * g:D_KV + HD * g + HD], k == 0, False)
                    ins = mm(banks[1][r, 0:HD], ptn[0:DEC_T, 1, r], vnew[0:DEC_T, b, 1, HD * g:HD * g + HD], False, True)
                ins.then_inc(sem("sa_ow"), 1)
            pe.wait_ge(sem("sa_out"), DEC_B // 2)
            for p_ in range(DEC_B // 2):
                ins = nc.tensor.transpose(banks[0][0:HD, p_ * P:(p_ + 1) * P], osum[:, p_, :], ident)
            ins.then_inc(once("so_turned")[0], 1)
            pe.wait_ge(*once("att_all_done"))
            pe.wait_ge(sem("rw_mixed"), NCH + 1)
            pe.wait_ge(sem("wo_in"), 16)
            for t in range(TILES + 1):
                if t < TILES:
                    n = rows(t)
                    if t >= 2:
                        pe.wait_ge(sem("h_ready"), t - 1)
                    for half in range(2):
                        for k in range(KT):
                            ins = mm(banks[2 * (t % 2) + half][0:n, :], mixed[:, k, t * P:t * P + n], wo[:, k, 512 * half:512 * half + 512],
                                     k == 0, k == KT - 1)
                    ins.then_inc(sem("h_mm"), 1)
                if t >= 1:
                    s = t - 1
                    n = rows(s)
                    pe.wait_ge(sem("hn_ready"), s + 1)
                    for half in range(2):
                        if s >= 1:
                            pe.wait_ge(sem("n2_out"), 2 * s + half - 1)
                        for k in range(4):
                            c = 4 * half + k
                            ins = nc.tensor.transpose(banks[4 + half][:, k * P:k * P + n], hn[0:n, c * P:(c + 1) * P], ident[0:n, 0:n])
                        ins.then_inc(sem("h_turned"), 1)
            pe.wait_ge(sem("n2_out"), 2 * TILES)
            for g in range(NG):
                pe.wait_ge(sem("wup_in"), 16 * (g + 1))
                for f in range(GF):
                    for s in range(3):
                        n = 3 * GF * g + 3 * f + s
                        if n >= 4:
                            pe.wait_ge(sem("relu"), n - 3)
                        a, w = SPANS[s]
                        for k in range(KT):
                            ins = mm(banks[n % 4][:, 0:w], wup[:, k, f * P:(f + 1) * P], mixed[:, k, a:a + w], k == 0, k == KT - 1)
                        ins.then_inc(sem("up"), 1)
                pe.wait_ge(sem("wdn_in"), 16 * (g + 1))
                pe.wait_ge(sem("squared"), 3 * GF * (g + 1))
                for t in range(TILES):
                    for half in range(2):
                        n = 2 * (TILES * g + t) + half
                        if n >= 4:
                            pe.wait_ge(sem("y_sum"), n - 3)
                        r = rows(t)
                        for f in range(GF):
                            lhs = act_p[:, f, t * P:(t + 1) * P] if t < PT else act_s[:, f, :]
                            ins = mm(banks[4 + n % 4][0:r, :], lhs, wdn[:, f, 512 * half:512 * half + 512], f == 0, f == GF - 1)
                        ins.then_inc(sem("down"), 1)

        @block.vector
        def _(dve):
            link = linker(dve, "dve_chain")
            tt, ts_, stt = nc.vector.tensor_tensor, nc.vector.tensor_scalar, nc.vector.scalar_tensor_tensor

            dve.wait_ge(sem("consts_in"), 16 * CONSTS)
            link(ts_(kav[:, 1, :], kav[:, 0, :], -1.0, 1.0, ALU.mult, ALU.add))
            dve.wait_ge(*once("iotas"))
            tss = nc.vector.tensor_single_scalar
            link(tss(it_col8, it_col, DEC_T - 1, ALU.bitwise_and))
            link(tss(it_col5, it_col, 5, ALU.logical_shift_right))
            link(tss(it_row2[:, 0:1], it_row, DEC_T - 1, ALU.bitwise_and))
            link(tss(it_row2[:, 1:2], it_row, 5, ALU.logical_shift_right))
            link(nc.vector.tensor_copy(col8, it_col8))
            link(nc.vector.tensor_copy(head_sum, it_col5))
            link(nc.vector.tensor_copy(row85, it_row2))
            link(ts_(head_sum, head_sum, row85[:, 1:2], None, ALU.is_equal))
            link(ts_(tail_add, col8[:, 0:DEC_T], row85[:, 0:1], NEG, ALU.is_gt, ALU.mult))
            link(ts_(first_add, col8[:, 0:DEC_T], row85[:, 0:1], NEG, ALU.is_le, ALU.mult))
            link(ts_(col8, col8, row85[:, 0:1], None, ALU.is_equal))
            link(tt(head_sum, head_sum, col8, ALU.mult))
            for t in range(TILES):
                n = rows(t)
                for half in range(2):
                    dve.wait_ge(sem("xn_turned"), 2 * t + half + 1)
                    src = shaped(banks[half], 4, P)[:, :, 0:n]
                    tt(nt[:, 4 * half:4 * half + 4, t * P:t * P + n], src,
                       spread(g1[:, 4 * half:4 * half + 4], 2, n), ALU.mult).then_inc(sem("nt_out"), 1)

            def head_norm(t):
                n = rows(t)
                heads = shaped(za[0:n, t, 0:D_ATTN], HEADS, HD)
                kv = shaped(za[0:n, t, D_ATTN:GATE0], 3, 2, KVH, HD)
                keys = kv[:, :, 0, :, :]
                dve.wait_ge(sem("proj_out"), att_done)
                link(tt(sq_a[0:n], heads, heads, ALU.mult))
                link(tt(sq_b[0:n], keys, keys, ALU.mult))
                link(nc.vector.tensor_reduce(head_rs[0:n, t % 2, 0:HEADS], sq_a[0:n], AX.X, ALU.add))
                nc.vector.tensor_reduce(head_rs[0:n, t % 2, HEADS:], sq_b[0:n].rearrange("p a b d -> p (a b) d"),
                                        AX.X, ALU.add).then_inc(sem("head_ss"), 1)
                link(tt(za[0:n, t, GATE0:], za[0:n, t, GATE0:], gb[0:n], ALU.add))
                dve.wait_ge(sem("head_rs"), t + 1)
                link(tt(heads, heads, spread(gq[0:n], 1, HEADS), ALU.mult))
                link(tt(heads, heads, spread(head_rs[0:n, t % 2, 0:HEADS], 2, HD), ALU.mult))
                for br in range(3):
                    kb = keys[:, br]
                    link(tt(kb, kb, spread(gk[0:n, br, :], 1, KVH), ALU.mult))
                    link(tt(kb, kb, spread(head_rs[0:n, t % 2, HEADS + 2 * br:HEADS + 2 * br + 2], 2, HD), ALU.mult))
                cos, sin = rope_t[0:n, t, 0, :], rope_t[0:n, t, 1, :]
                parts = [(heads, HEADS)] + [(keys[:, br], KVH) for br in range(3)]
                last = parts[-1][0]
                for v, h in parts:
                    a_, b_ = ra[0:n, 0:h, :], rb[0:n, 0:h, :]
                    link(tt(a_, v[:, :, 0:ROT], spread(cos, 1, h), ALU.mult))
                    link(tt(b_[:, :, 0:8], v[:, :, 8:16], spread(sin[:, 0:8], 1, h), ALU.mult))
                    link(tt(b_[:, :, 8:16], v[:, :, 0:8], spread(sin[:, 8:16], 1, h), ALU.mult))
                    ins = tt(v[:, :, 0:ROT], a_, b_, ALU.add)
                    if v is not last:
                        link(ins)
                ins.then_inc(sem("kv_final"), 1)

            for t in range(TILES):
                head_norm(t)
            dve.wait_ge(sem("proj_out"), len(PROJ))
            dve.wait_ge(*once("shift_turned"))
            link(nc.vector.tensor_copy(zs[:, :, :, 0], shaped(banks[0][:, 0:RC * DEC_B], RC, DEC_B)))
            link(nc.vector.tensor_copy(last_cols[:, :, 0:DEC_B], zs[:, :, :, DEC_T]))
            nc.vector.tensor_copy(last_cols[:, :, DEC_B:], rt[:, :, SEQ:]).then_inc(once("last_cols")[0], 1)
            dve.wait_ge(*once("last_turned"))
            for q in range(4):
                w = min(512, ZR - 512 * q)
                ins = nc.vector.tensor_copy(shift_rows[0:DEC_B + 1, 512 * q:512 * q + w], banks[4 + q][0:DEC_B + 1, 0:w])
                if q < 3:
                    link(ins)
            ins.then_inc(once("shift_out")[0], 1)

            dve.wait_ge(sem("shift_stored"), 32)
            dve.wait_ge(*once("masks_ready"))
            nc.vector.memset(st, 0.0).then_inc(once("rw_st0")[0], 1)

            def f_dve(c):
                smp, r = int(c == NCH), c % 3
                pr, atrb, gtrk, tu, dec = pr_r[r], atrb_r[r], gtrk_r[r], tu_r[r], dec_r[r]
                if smp:
                    cur, prev = zs[:, :, :, 1:], zs[:, :, :, 0:DEC_T]
                    xv = xs.rearrange("p a (b c) -> p a b c", b=DEC_B)
                else:
                    cur, prev, xv = rt[:, :, 1 + CH * c:1 + CH * c + CH], rt[:, :, CH * c:CH * c + CH], xs
                link(tt(xv, prev, cur, ALU.subtract))
                link(tt(xs, xs, spread(mu, 2, CH), ALU.mult))
                yield
                tt(xv, xv, cur, ALU.add).then_inc(sem("rw_xs"), 1)
                dve.wait_ge(sem("rw_xs"), c + 1)
                if c == NCH - 1:
                    nc.vector.engine_nop().then_inc(once("rw_prompt_done")[0], 1)
                tt(kkraw, xs[:, 4:8, :], spread(kkv, 2, CH), ALU.mult).then_inc(sem("rw_kkraw"), 1)
                yield
                dve.wait_ge(sem("rw_e"), c + 1)
                link(ts_(ebuf, ebuf, 1.0, None, ALU.add))
                link(nc.vector.reciprocal(ebuf, ebuf))
                link(ts_(lbuf, ebuf, e_scale[:, 1:2], e_scale[:, 2:3], ALU.mult, ALU.add))
                nc.vector.tensor_copy(lbuf[32:64, :], xs[32:64, 12, :]).then_inc(sem("rw_l"), 1)
                yield
                yield
                dve.wait_ge(sem("rw_wa"), c + 1)
                for q in range(2):
                    ins = tt(sig[:, q], shaped(banks[q][:, 0:256], HP, CH),
                             spread(w0a0[:, q * HP:(q + 1) * HP], 2, CH), ALU.add)
                ins.then_inc(sem("rw_u"), 1)
                ts_(ssm, shaped(banks[0][:, 256:512], HP, CH), 1e-24, None, ALU.max).then_inc(sem("rw_ssm"), 1)
                yield
                dve.wait_ge(sem("rw_esig"), c + 1)
                link(ts_(sig, sig, 1.0, None, ALU.add))
                link(nc.vector.reciprocal(sig[:, 0], sig[:, 0]))
                yield
                link(nc.vector.tensor_tensor_scan(cs.rearrange("p a b -> p (a b)"), scan_keep[:, smp, :],
                                                  sig[:, 0].rearrange("p a b -> p (a b)"), 0.0, ALU.mult, ALU.add))
                tt(cx, cs, sig[:, 0], ALU.subtract).then_inc(sem("rw_cs"), 1)
                link(nc.vector.reciprocal(sig[:, 1], sig[:, 1]))
                yield
                dve.wait_ge(sem("rw_rs"), c + 1)
                link(stt(kkn, kkraw, 2.0 ** 15, ssm, ALU.mult, ALU.mult))
                link(tt(kka, kkn, sig[:, 1], ALU.mult))
                yield
                if c > 0:
                    dve.wait_ge(sem("rw_tok"), c)
                link(tt(tmp, sig[:, 1], spread(kav[:, 0, :], 2, CH), ALU.mult))
                link(tt(tmp, tmp, spread(kav[:, 1, :], 2, CH), ALU.add))
                link(tt(kmod, xs[:, 4:8, :], tmp, ALU.mult))
                yield
                link(tt(rkk, xs[:, 0:4, :], kmod, ALU.mult))
                link(tt(rkk, rkk, spread(rkv, 2, CH), ALU.mult))
                yield
                dve.wait_ge(sem("rw_dec"), c + 1)
                link(tt(pr[:, :, 0, :], kkn, dprev, ALU.mult))
                link(tt(bk[:, :, 0, :], kka, dinv, ALU.mult))
                link(tt(bk[:, :, 1, :], kmod, dinv, ALU.mult))
                tt(pr[:, :, 1, :], xs[:, 0:4, :], dec, ALU.mult).then_inc(sem("rw_prbk"), 1)
                yield
                yield
                dve.wait_ge(sem("rw_prod"), c + 1)
                msk = spread(m_t[:, smp].rearrange("p a b -> p (a b)"), 1, HP)
                tt(atrb.rearrange("p a b c -> p a (b c)"), shaped(banks[0], HP, P), msk, ALU.mult).then_inc(sem("rw_prod_sb"), 1)
                yield
                link(tt(gtrk.rearrange("p a b c -> p a (b c)"), shaped(banks[1], HP, P), msk, ALU.mult))
                link(tt(amat, shaped(banks[2][:, 0:256], HP, CH), spread(m_a[:, smp, :], 1, HP), ALU.mult))
                link(nc.vector.tensor_copy(bonus_r[r], banks[2][:, 256:256 + HP]))
                yield
                dve.wait_ge(sem("rw_prod_sb"), c + 1)
                link(tt(tu[:, :, 0, :], amat, spread(m_one, 1, HP), ALU.mult))
                link(tt(tu[:, :, 1, :], atrb[:, :, 0, :], spread(m_onet, 1, HP), ALU.mult))
                yield
                for h in HALVES:
                    eye = spread(spread(ident[h, h], 1, 2), 1, HP)
                    ins = tt(tu[h], eye, tu[h], ALU.subtract)
                    if h is HALVES[0]:
                        link(ins)
                ins.then_inc(sem("rw_ti"), 1)
                yield

            def l_dve(c):
                tu = tu_r[c % 3]
                for i in range(len(LEVELS)):
                    yield
                    if i < nlev(c):
                        dve.wait_ge(sem("rw_tx"), lev0(c) + i + 1)
                        if i < nlev(c) - 1:
                            flat = tu.rearrange("p a b c -> p (a b c)")
                            tt(flat, flat, banks[4], ALU.subtract).then_inc(sem("rw_t"), 1)
                        else:
                            tt(tu[:, :, 1, :], tu[:, :, 1, :], shaped(banks[4], HP, 2, CH)[:, :, 1, :], ALU.subtract).then_inc(sem("rw_t"), 1)
                    yield

            def y_dve(c):
                smp, r = int(c == NCH), c % 3
                vtok, gtok, bonus, dec = vtok_r[r], gtok_r[r], bonus_r[r], dec_r[r]
                yield
                dve.wait_ge(sem("rw_uu"), c + 1)
                if not smp:
                    ts_(nu, shaped(banks[5][:, 256:512], HP, CH), -1.0, None, ALU.mult).then_inc(sem("rw_nu"), 1)
                else:
                    link(ts_(nu, shaped(banks[5][:, 256:512], HP, CH), -1.0, None, ALU.mult))
                    for hp in range(HP):
                        rowm = spread(row_of, 2, HD)
                        link(tt(nub[:, hp], spread(nu[:, hp, :], 1, DEC_B), rowm, ALU.mult))
                        ins = tt(vb[:, hp], spread(vtok[:, hp, :], 1, DEC_B), rowm, ALU.mult)
                        if hp < HP - 1:
                            link(ins)
                    ins.then_inc(sem("rw_nu"), 1)
                yield
                dve.wait_ge(sem("rw_y"), c + 1)
                if smp:
                    for hp, q in enumerate(SBANK):
                        link(tt(sst[:, hp], sst[:, hp], shaped(banks[q], DEC_B, HD), ALU.add))
                        end = dec[:, hp, DEC_T - 1::DEC_T]
                        ins = tt(sst[:, hp], sst[:, hp], spread(end, 2, HD), ALU.mult)
                        if hp < HP - 1:
                            link(ins)
                    ins.then_inc(sem("rw_st"), 1)
                else:
                    link(tt(st, st, shaped(banks[6][:, 0:256], HP, HD), ALU.add))
                    tt(st, st, spread(dec[:, :, CH - 1], 2, HD), ALU.mult).then_inc(sem("rw_st"), 1)
                yield
                y = shaped(banks[6][:, 256:512], HP, HD)
                link(nc.vector.tensor_reduce(ystat[:, 0, :], y, AX.X, ALU.add))
                link(ts_(ystat[:, 0, :], ystat[:, 0, :], 1.0 / HD, None, ALU.mult))
                link(tt(yc, y, spread(ystat[:, 0, :], 2, HD), ALU.subtract))
                link(tt(sqy, yc, yc, ALU.mult))
                nc.vector.tensor_reduce(ystat[:, 1, :], sqy, AX.X, ALU.add).then_inc(sem("rw_var"), 1)
                yield
                link(tt(yc, yc, lnw, ALU.mult))
                link(tt(bv, vtok, spread(bonus, 2, HD), ALU.mult))
                link(tt(bv, bv, lnb, ALU.add))
                dve.wait_ge(sem("rw_yrs"), c + 1)
                link(tt(yc, yc, spread(ystat[:, 1, :], 2, HD), ALU.mult))
                link(tt(yc, yc, bv, ALU.add))
                tt(yc, yc, gtok, ALU.mult).then_inc(sem("rw_yo"), 1)
                yield
                yield

            staged(f_dve, l_dve, y_dve)
            dve.wait_ge(sem("rw_sstate"), DEC_B)
            dve.wait_ge(sem("rw_mixed"), NCH + 1)
            dve.wait_ge(sem("rw_yt"), NCH + 1)
            nc.vector.engine_nop().then_inc(once("rw_all_done")[0], 1)
            dve.wait_ge(*once("egates"))
            link(ts_(gates[:, 0:PT], gates[:, 0:PT], 1.0, None, ALU.add))
            link(ts_(gates[0:NS, PT], gates[0:NS, PT], 1.0, None, ALU.add))
            link(nc.vector.reciprocal(gates[:, 0:PT], gates[:, 0:PT]))
            link(nc.vector.reciprocal(gates[0:NS, PT], gates[0:NS, PT]))
            dve.wait_ge(*once("pe_sum"))
            pes = shaped(banks[5][:, 0:4], 2, 2)
            link(nc.vector.tensor_copy(pebias[0:64], pes[0:64, :, 0]))
            nc.vector.tensor_copy(pebias[64:128], pes[64:128, :, 1]).then_inc(once("pe_bias")[0], 1)
            dve.wait_ge(*once("pe_bias"))

            def key_rows(u):
                dve.wait_ge(sem(f"chunk_in{u % 2}"), chunk_loads(u))
                nc.vector.tensor_copy(*head_rows(u, 0)).then_inc(sem("cm_krows"), 1)

            key_rows(0)
            for u in range(NSEQ):
                n = SEQ // STRIDE if u == 0 else P
                for f in range(0, 8, 2):
                    g = 8 * u + f
                    dve.wait_ge(sem("cm_turned"), g + 1)
                    if g >= 4:
                        dve.wait_ge(sem("cm_mm"), g - 3)
                    nc.vector.tensor_copy(xt[g % 4][:, :, :, 0:n], shaped(banks[g % 4], 2, KVH, P)[:, :, :, 0:n]).then_inc(sem("cm_x0"), 1)
                    if f == 4 and u + 1 < NSEQ:
                        key_rows(u + 1)
                dve.wait_ge(sem("cm_mm"), 8 * (u + 1))
                if u > 0:
                    dve.wait_ge(sem("cm_sel"), u)
                for c in range(2):
                    ins = ts_(ycmp[:, c, :, 0:n], shaped(banks[4 + c][:, 0:KVH * n], KVH, n), pebias[:, c:c + 1], None, ALU.add)
                    if c == 0:
                        link(ins)
                ins.then_inc(sem("cm_y"), 1)
            dve.wait_ge(sem("cm_kv"), NSEQ)
            for slot in range(2):
                for g in range(KVH):
                    ins = nc.vector.memset(qt[slot][HALVES[1 - g], g], 0.0)
            ins.then_inc(once("q_zero")[0], 1)

            def acc_unit(u):
                i, kind, h = units[u]
                dve.wait_ge(sem("pa_o"), u + 1)
                if kind == "c":
                    if i >= 2:
                        f = turn_no[("m", i - 2)]
                        dve.wait_ge(sem("turn_in"), f + 1)
                    link(nc.vector.reciprocal(c8[:, 1, :], c8[:, 1, :]))
                    link(tt(c8[:, 1, :], c8[:, 1, :], gates[:, i, 0::3], ALU.mult))
                    tt(oacc[i % 2], shaped(banks[6 + u % 2], HEADS, HD), spread(c8[:, 1, :], 2, HD), ALU.mult).then_inc(sem("pa_acc"), 1)
                else:
                    w = psum_[:, u % 4:u % 4 + 1]
                    link(nc.vector.reciprocal(w, w))
                    br = 1 if kind == "s" else 2
                    link(tt(w, w, gates[:, i, 3 * h + br:3 * h + br + 1], ALU.mult))
                    dve.wait_ge(sem("pa_acc"), u)
                    stt(oacc[i % 2][:, h, :], banks[6 + u % 2][:, 0:HD], w, oacc[i % 2][:, h, :], ALU.mult, ALU.add).then_inc(sem("pa_acc"), 1)

            for e in events:
                if e[0] in "qTm":
                    f = turn_no[e]
                    if f % 2 == 0:
                        dve.wait_ge(sem("turn_in"), f + 1)
                        turn_copy(e, dve, lambda out, in_, scale: (nc.vector.tensor_copy(out, in_) if scale == 1.0 else
                                                                   ts_(out, in_, scale, None, ALU.mult))).then_inc(sem("turn_out0"), 1)
                elif e[0] == "S":
                    u = e[1]
                    i, kind, h = units[u]
                    dve.wait_ge(sem("pa_s"), u + 1)
                    s0 = 1024 * (u % 2)
                    if kind == "c":
                        if u >= 2:
                            dve.wait_ge(sem("pa_t"), u - 1)
                        pc = shaped(pbuf[u % 2][:, 0:HEADS * NCMP_P], HEADS, NCMP_P)
                        for g in range(KVH):
                            sc = shaped(psum[:, s0 + 512 * g:s0 + 512 * g + HG * NCMP_P], HG, NCMP_P)
                            link(tt(pc[:, HG * g:HG * (g + 1)], sc, spread(cmp_add[:, i, :], 1, HG), ALU.add))
                        link(nc.vector.tensor_reduce(c8[:, 0, :], pc, AX.X, ALU.max))
                        tt(pc, pc, spread(c8[:, 0, :], 2, NCMP_P), ALU.subtract).then_inc(sem("pa_max"), 1)
                        dve.wait_ge(sem("pa_p"), u + 1)
                        link(nc.vector.tensor_reduce(c8[:, 1, :], pc, AX.X, ALU.add))
                        tt(pc, pc, spread(cmp_keep[:, i, :], 1, HEADS), ALU.mult).then_inc(sem("pa_pm"), 1)
                    else:
                        ks = key_tiles(u)
                        n = P * len(ks)
                        last = psum[:, s0 + n - P:s0 + n]
                        link(tt(last, last, causal_add, ALU.add))
                        if kind == "w" and i >= WINDOW // P:
                            first = psum[:, s0:s0 + P]
                            link(tt(first, first, edge_add, ALU.add))
                        nc.vector.tensor_reduce(pmax[:, u % 4:u % 4 + 1], psum[:, s0:s0 + n], AX.X, ALU.max, negate=True).then_inc(sem("pa_max"), 1)
                elif e[0] == "O":
                    acc_unit(e[1])
            dve.wait_ge(sem("turn_in"), len(turns))
            dve.wait_ge(sem("turn_out1"), len(turns) // 2)
            nc.vector.engine_nop().then_inc(once("pa_done")[0], 1)
            dve.wait_ge(*once("gs_spread"))
            for p_ in range(DEC_B // 2):
                link(tt(gtmp, banks[1][:, p_ * P:p_ * P + 3 * HEADS].rearrange("p (h r) -> p r h", r=3), spread(row_of, 1, 3), ALU.mult))
                link(nc.vector.tensor_reduce(gs[:, p_, :], gtmp, AX.X, ALU.add))
            link(nc.vector.memset(pcs, 0.0))
            for p_ in range(DEC_B // 2):
                dve.wait_ge(sem("sc_s"), p_ + 1)
                nc.vector.tensor_reduce(sst4[:, 0:1], banks[0][:, 0:NCMP], AX.X, ALU.max, negate=True).then_inc(sem("sc_max"), 1)
                dve.wait_ge(sem("sc_p"), p_ + 1)
                link(nc.vector.reciprocal(sst4[:, 1:2], sst4[:, 1:2]))
                ts_(pcs[:, 1:1 + NCMP], pcs[:, 1:1 + NCMP], sst4[:, 1:2], None, ALU.mult).then_inc(sem("sc_pn"), 1)
                dve.wait_ge(sem("sc_t"), p_ + 1)
                link(nc.vector.tensor_copy(ptn_c[0:NCMP, :], banks[4][0:NCMP, 0:P]))
                dve.wait_ge(sem("sc_hs"), p_ + 1)
                link(nc.vector.tensor_copy(pcs[:, 1:1 + NCMP], banks[7][:, 0:NCMP]))
                link(nc.vector.tensor_reduce(imp[:, 0:NBLK - 1], shaped(pcs[:, 0:P], NBLK - 1, SLC // STRIDE), AX.X, ALU.add))
                link(tt(imp[:, 0:NBLK - 1], imp[:, 0:NBLK - 1], pcs[:, SLC // STRIDE::SLC // STRIDE], ALU.add))
                link(nc.vector.memset(imp[:, 0:1], 1e9))
                link(nc.vector.memset(imp[:, NBLK - 2:], 1e9))
                big, eq = rank_gt, rank_eq
                link(tt(big, spread(imp, 1, NBLK), spread(imp, 2, NBLK), ALU.is_gt))
                link(tt(eq, spread(imp, 1, NBLK), spread(imp, 2, NBLK), ALU.is_equal))
                link(tt(eq, eq, before, ALU.mult))
                link(tt(big, big, eq, ALU.add))
                link(nc.vector.tensor_reduce(imp, big, AX.X, ALU.add))
                link(ts_(imp, imp, float(NSEL), 1.0, ALU.is_lt, ALU.subtract))
                ts_(imp, imp, -NEG, None, ALU.mult).then_inc(sem("sc_ptr"), 1)
                for bb in range(2):
                    b = 2 * p_ + bb
                    dve.wait_ge(sem("ctok_in"), 16 * NPG * (b + 1))
                    dve.wait_ge(sem("sk_turned"), 4 * (b + 1))
                    nc.vector.tensor_copy(vtok2[:, bb], ctok[:, :, D_KV:]).then_inc(sem("sa_vcopied"), 1)
                dve.wait_ge(sem("sc_ptr"), p_ + 1)
                dve.wait_ge(sem("ss_s"), 2 * p_ + 2)
                for q in range(4):
                    link(tt(shaped(ssel[:, 512 * q:512 * q + 512], 8, SLC), shaped(banks[q], 8, SLC), spread(imp[:, 8 * q:8 * q + 8], 2, SLC), ALU.add))
                link(tt(ssel[:, PAST:], banks[4][:, 0:DEC_T], tail_add, ALU.add))
                nc.vector.tensor_reduce(sst4[:, 0:1], ssel, AX.X, ALU.max, negate=True).then_inc(sem("ss_max"), 1)
                dve.wait_ge(sem("sa_oc"), p_ + 1)
                ts_(osum[:, p_, :], banks[7][:, 0:HD], gs[:, p_, 0:1], None, ALU.mult).then_inc(sem("sa_acc_c"), 1)
                for q in range(0, 4, 2):
                    dve.wait_ge(sem("sp_turned"), 6 * p_ + q + 1)
                    nc.vector.tensor_copy(ktb[:, 512 * q:512 * q + 512], banks[q]).then_inc(sem("sp_dve"), 1)
                dve.wait_ge(sem("sp_turned"), 6 * p_ + 5)
                nc.vector.tensor_copy(ptn[0:DEC_T, 0, :], banks[4][0:DEC_T, 0:P]).then_inc(sem("sp_ptn"), 1)
                dve.wait_ge(sem("swk_turned"), p_ + 1)
                for bb in range(2):
                    ins = nc.vector.tensor_copy(swk[bb], banks[5 + bb])
                    if bb == 0:
                        link(ins)
                ins.then_inc(sem("swk_ready"), 1)
                dve.wait_ge(sem("sw_s"), p_ + 1)
                dve.wait_ge(sem("ss_p"), p_ + 1)
                link(tt(swin[:, 0:DEC_T], banks[7][:, 0:DEC_T], first_add, ALU.add))
                link(nc.vector.tensor_copy(swin[:, DEC_T:WINDOW], banks[7][:, DEC_T:]))
                link(tt(swin[:, WINDOW:], banks[4][:, 0:DEC_T], tail_add, ALU.add))
                nc.vector.tensor_reduce(sst4[:, 0:1], swin, AX.X, ALU.max, negate=True).then_inc(sem("sw_max"), 1)
                dve.wait_ge(sem("sw_p"), p_ + 1)
                link(nc.vector.reciprocal(sst4[:, 2:4], sst4[:, 2:4]))
                link(tt(sst4[:, 2:4], sst4[:, 2:4], gs[:, p_, 1:3], ALU.mult))
                dve.wait_ge(sem("sa_acc_c"), p_ + 1)
                dve.wait_ge(sem("sa_os"), p_ + 1)
                link(stt(osum[:, p_, :], banks[0][:, 0:HD], sst4[:, 2:3], osum[:, p_, :], ALU.mult, ALU.add))
                dve.wait_ge(sem("sa_ow"), p_ + 1)
                stt(osum[:, p_, :], banks[1][:, 0:HD], sst4[:, 3:4], osum[:, p_, :], ALU.mult, ALU.add).then_inc(sem("sa_out"), 1)
            def n2_out(t):
                n = rows(t)
                for half in range(2):
                    dve.wait_ge(sem("h_turned"), 2 * t + half + 1)
                    tt(mixed[:, 4 * half:4 * half + 4, t * P:t * P + n], shaped(banks[4 + half], 4, P)[:, :, 0:n],
                       spread(g2n[:, 4 * half:4 * half + 4], 2, n), ALU.mult).then_inc(sem("n2_out"), 1)

            for t in range(TILES):
                n = rows(t)
                dve.wait_ge(sem("h_mm"), t + 1)
                dve.wait_ge(sem(f"x2_in{t % 2}"), 16 * (t // 2 + 1))
                tt(y[0:n, t, :], psum[0:n, 1024 * (t % 2):1024 * (t % 2) + 1024], x2[t % 2][0:n], ALU.add).then_inc(sem("h_ready"), 1)
                if t >= 1:
                    n2_out(t - 1)
            n2_out(TILES - 1)
            for g in range(NG):
                for j in range(3 * GF):
                    f, s = divmod(j, 3)
                    n = 3 * GF * g + j
                    dve.wait_ge(sem("relu"), n + 1)
                    tt(act_of(f, s), act_of(f, s), act_of(f, s), ALU.mult).then_inc(sem("squared"), 1)
                for t in range(TILES):
                    for half in range(2):
                        n = 2 * (TILES * g + t) + half
                        r = rows(t)
                        dve.wait_ge(sem("down"), n + 1)
                        yh = y[0:r, t, 512 * half:512 * half + 512]
                        if g > 0:
                            dve.wait_ge(sem("y_sum"), n - 2 * TILES + 1)
                        tt(yh, yh, banks[4 + n % 4][0:r, :], ALU.add).then_inc(sem("y_sum"), 1)


_INS = ['x_prompt', 'x_sample', 'cache_cmp_kv', 'cache_slc_kv', 'cache_win_kv', 'state_wkv', 'state_shift',
        'page_table', 'norm1_g', 'w_in', 'q_norm_g', 'k_norm_g', 'gate_b', 'cmp_pe', 'cmp_w', 'shift_mu', 'w0',
        'w2', 'a0', 'a2', 'g2', 'k_k', 'k_a', 'r_k', 'lnx_w', 'lnx_b', 'w_out', 'norm2_g', 'w_up', 'w_down']
_KV = (2, KVH, HD)
_OUTS = [(1, SEQ, D_MODEL), (DEC_B, DEC_T, D_MODEL),
         (1, 1, PT, PAGE) + _KV, (1, 1, PT, PAGE) + _KV, (1, 1, WINDOW) + _KV,
         (1, 1, HEADS, HD, HD), (1, 1, ZR),
         (1, DEC_B, DEC_T) + _KV, (1, DEC_B, DEC_T) + _KV, (1, DEC_B, WINDOW) + _KV,
         (1, DEC_B, HEADS, HD, HD), (1, DEC_B, ZR)]


def _rope_table():
    import numpy as np
    inv = np.power(np.float32(500000.0), -(np.arange(0, ROT, 2, dtype=np.float32) / np.float32(ROT)))
    pos = np.zeros((TILES, P), np.float32)
    pos[:PT] = np.arange(SEQ, dtype=np.float32).reshape(PT, P)
    pos[PT, :NS] = np.tile(PAST + np.arange(DEC_T, dtype=np.float32), DEC_B)
    angle = pos[..., None] * inv
    cos, sin = np.cos(angle), np.sin(angle)
    return np.stack([np.concatenate([cos, cos], -1), np.concatenate([-sin, sin], -1)], 2).astype(np.float32)


def kernel(**inputs):
    import numpy as _np
    import concourse.bacc as _bacc
    from concourse import mybir as _mybir
    from concourse.bass_utils import run_bass_kernel_spmd as _run

    nc = _bacc.Bacc("TRN2", target_bir_lowering=False, num_devices=1)
    arrays, args = {}, []
    laid = {name: _np.ascontiguousarray(inputs[name]) for name in _INS}
    laid["rope"] = _rope_table()
    for name, a in laid.items():
        arrays[f"in_{name}_dram"] = a
        args.append(nc.dram_tensor(f"in_{name}_dram", a.shape, _mybir.dt.from_np(a.dtype), kind="ExternalInput").ap())
    for i, shape in enumerate(_OUTS):
        args.append(nc.dram_tensor(f"out_{i}_dram", shape, _mybir.dt.float32, kind="ExternalOutput").ap())
    decode_trunk(nc, *args)
    r = _run(nc, [arrays], core_ids=[0])
    return tuple(r.results[0][f"out_{i}_dram"] for i in range(len(_OUTS)))
```
